# Optimizing a Trainium2 kernel written in Bass

```python
import jax, jax.numpy as jnp
from jax import lax
import numpy as np

D_MODEL = 1024
BATCH = 1
SEQ = 512
DEPTH = 2
DEC_BATCH = 1
DEC_SEQ = 64
PAST_LEN = 256

CHUNK = 64
WINDOW = 128
WIN_CHUNKS = WINDOW // CHUNK
HEAD_DIM = 64
N_Q_HEADS = 8
N_KV_HEADS = 2
Q_PER_KV = N_Q_HEADS // N_KV_HEADS
ATT_WIDTH = N_Q_HEADS * HEAD_DIM
KV_WIDTH = N_KV_HEADS * HEAD_DIM
ROPE_THETA = 10000.0
GM_GROUPS = 4
GM_CH = 128
GM_WIDTH = GM_GROUPS * GM_CH
GM_CHUNK = 128
D_MIX = ATT_WIDTH + GM_WIDTH
D_IN = ATT_WIDTH + 2 * KV_WIDTH + 2 * GM_WIDTH
N_EXPERTS = 16
N_EXPERT_GROUPS = 4
EXPERTS_PER_GROUP = N_EXPERTS // N_EXPERT_GROUPS
TOP_K = 2
D_EXPERT = 512
ALPHA = (2 * DEPTH) ** 0.25
BETA = (8 * DEPTH) ** -0.25
LN_EPS = 1e-5
NEG_INF = -1e30

kernel_name = "hymba_swa_sink_gmlp_grouped_moe_stream_step"

def layer_norm(x, g, b):
    xf = x.astype(jnp.float32)
    mu = xf.mean(-1, keepdims=True)
    var = jnp.square(xf - mu).mean(-1, keepdims=True)
    y = (xf - mu) * lax.rsqrt(var + LN_EPS) * g.astype(jnp.float32) + b.astype(jnp.float32)
    return y.astype(x.dtype)

def rms_norm(x, g):
    xf = x.astype(jnp.float32)
    y = xf * lax.rsqrt(jnp.square(xf).mean(-1, keepdims=True) + LN_EPS) * g.astype(jnp.float32)
    return y.astype(x.dtype)

def rope(x, pos):
    half = HEAD_DIM // 2
    inv = ROPE_THETA ** (-jnp.arange(half, dtype=jnp.float32) / half)
    ang = pos.astype(jnp.float32)[:, None] * inv[None, :]
    cos = jnp.cos(ang)[:, None, :]
    sin = jnp.sin(ang)[:, None, :]
    x1 = x[..., :half].astype(jnp.float32)
    x2 = x[..., half:].astype(jnp.float32)
    return jnp.concatenate([x1 * cos - x2 * sin, x2 * cos + x1 * sin], -1).astype(x.dtype)

def split_proj(x, w_in):
    h = jnp.einsum('bsd,de->bse', x, w_in)
    o1 = ATT_WIDTH
    o2 = o1 + KV_WIDTH
    o3 = o2 + KV_WIDTH
    o4 = o3 + GM_WIDTH
    B, S = x.shape[:2]
    q = h[..., :o1].reshape(B, S, N_Q_HEADS, HEAD_DIM)
    k = h[..., o1:o2].reshape(B, S, N_KV_HEADS, HEAD_DIM)
    v = h[..., o2:o3].reshape(B, S, N_KV_HEADS, HEAD_DIM)
    return q, k, v, h[..., o3:o4], h[..., o4:]

def sink_attention(q, k, v, sinks, mask):
    s = jnp.einsum('...qhgd,...khd->...hgqk', q, k).astype(jnp.float32) * (HEAD_DIM ** -0.5)
    if mask is not None:
        s = jnp.where(mask, s, NEG_INF)
    sink = jnp.broadcast_to(sinks.astype(jnp.float32).reshape(N_KV_HEADS, Q_PER_KV, 1, 1), s.shape[:-1] + (1,))
    p = jax.nn.softmax(jnp.concatenate([s, sink], -1), axis=-1)[..., :-1]
    return jnp.einsum('...hgqk,...khd->...qhgd', p.astype(v.dtype), v)

def window_attention_prompt(q, k, v, sinks):
    B, S = q.shape[:2]
    nc = S // CHUNK
    qb = q.reshape(B, nc, CHUNK, N_KV_HEADS, Q_PER_KV, HEAD_DIM)
    pad = ((0, 0), (WIN_CHUNKS * CHUNK, 0), (0, 0), (0, 0))
    kp = jnp.pad(k, pad).reshape(B, nc + WIN_CHUNKS, CHUNK, N_KV_HEADS, HEAD_DIM)
    vp = jnp.pad(v, pad).reshape(B, nc + WIN_CHUNKS, CHUNK, N_KV_HEADS, HEAD_DIM)
    kb = jnp.concatenate([kp[:, i:i + nc] for i in range(WIN_CHUNKS + 1)], axis=2)
    vb = jnp.concatenate([vp[:, i:i + nc] for i in range(WIN_CHUNKS + 1)], axis=2)
    blk = jnp.arange(nc)[:, None] + jnp.arange((WIN_CHUNKS + 1) * CHUNK)[None, :] // CHUNK - WIN_CHUNKS
    mask = (blk >= 0)[:, None, None, None, :]
    o = sink_attention(qb, kb, vb, sinks, mask)
    return o.reshape(B, S, ATT_WIDTH)

def window_attention_sample(q, k_new, v_new, k_cache, v_cache, sinks):
    B, T = q.shape[:2]
    qb = q.reshape(B, T, N_KV_HEADS, Q_PER_KV, HEAD_DIM)
    k_all = jnp.concatenate([k_cache, k_new], axis=1)
    v_all = jnp.concatenate([v_cache, v_new], axis=1)
    o = sink_attention(qb, k_all, v_all, sinks, None)
    return o.reshape(B, T, ATT_WIDTH)

def gmlp_prompt(u, gv, ln_g, ln_b, ws, bs):
    B, S = u.shape[:2]
    n = S // GM_CHUNK
    ug = jax.nn.gelu(u, approximate=False).reshape(B, n, GM_CHUNK, GM_GROUPS, GM_CH)
    vn = layer_norm(jax.nn.gelu(gv, approximate=False).reshape(B, n, GM_CHUNK, GM_GROUPS, GM_CH), ln_g, ln_b)
    s = jnp.einsum('gpq,bnqgc->bnpgc', jnp.tril(ws), vn) + bs.T[:, :, None]
    return (ug * s).reshape(B, S, GM_WIDTH)

def gmlp_sample(u, gv, ln_g, ln_b, ws, bs):
    B, T = u.shape[:2]
    ug = jax.nn.gelu(u, approximate=False).reshape(B, T, GM_GROUPS, GM_CH)
    vn = layer_norm(jax.nn.gelu(gv, approximate=False).reshape(B, T, GM_GROUPS, GM_CH), ln_g, ln_b)
    s = jnp.einsum('gpq,bqgc->bpgc', jnp.tril(ws)[:, :T, :T], vn) + bs[:, :T].T[:, :, None]
    return (ug * s).reshape(B, T, GM_WIDTH), vn.reshape(B, T, GM_WIDTH)

def grouped_moe(x, w_router, router_bias, wg, wu, wd):
    shp = x.shape
    xt = x.reshape(-1, D_MODEL)
    scores = jax.nn.sigmoid(jnp.einsum('td,de->te', xt.astype(jnp.float32), w_router.astype(jnp.float32)))
    sel = scores + router_bias.astype(jnp.float32)
    grp_score = lax.top_k(sel.reshape(-1, N_EXPERT_GROUPS, EXPERTS_PER_GROUP), 2)[0].sum(-1)
    best = jnp.argmax(grp_score, axis=-1)
    in_grp = (jnp.arange(N_EXPERTS) // EXPERTS_PER_GROUP)[None, :] == best[:, None]
    _, idx = lax.top_k(jnp.where(in_grp, sel, NEG_INF), TOP_K)
    w = jnp.take_along_axis(scores, idx, axis=-1)
    w = w / w.sum(-1, keepdims=True)
    combine = jnp.einsum('tk,tke->te', w, jax.nn.one_hot(idx, N_EXPERTS, dtype=jnp.float32)).astype(x.dtype)
    y = jnp.zeros_like(xt)
    for e in range(N_EXPERTS):
        h = jax.nn.silu(xt @ wg[e]) * (xt @ wu[e])
        y = y + combine[:, e:e + 1] * (h @ wd[e])
    return y.reshape(shp)

def setup_inputs(seed: int = 0) -> dict:
    key = jax.random.key(seed)
    ks = jax.random.split(key, 24)
    f32 = jnp.float32
    n = lambda k, s: jax.random.normal(k, s, f32)
    cache_len = min(WINDOW, PAST_LEN)
    col_scale = jnp.concatenate([
        jnp.ones((ATT_WIDTH + KV_WIDTH,), f32), jnp.full((KV_WIDTH,), BETA, f32),
        jnp.full((GM_WIDTH,), BETA, f32), jnp.ones((GM_WIDTH,), f32)])
    return {
        "x_prompt": n(ks[0], (BATCH, SEQ, D_MODEL)),
        "x_sample": n(ks[1], (DEC_BATCH, DEC_SEQ, D_MODEL)),
        "cache_k": n(ks[2], (DEPTH, DEC_BATCH, cache_len, N_KV_HEADS, HEAD_DIM)),
        "cache_v": n(ks[3], (DEPTH, DEC_BATCH, cache_len, N_KV_HEADS, HEAD_DIM)),
        "w_in": n(ks[4], (DEPTH, D_MODEL, D_IN)) * (D_MODEL ** -0.5) * col_scale,
        "sinks": 0.5 * n(ks[5], (DEPTH, N_Q_HEADS)),
        "gm_ln_g": 1.0 + 0.02 * n(ks[6], (DEPTH, GM_GROUPS, GM_CH)),
        "gm_ln_b": 0.02 * n(ks[7], (DEPTH, GM_GROUPS, GM_CH)),
        "gm_ws": n(ks[8], (DEPTH, GM_GROUPS, GM_CHUNK, GM_CHUNK)) * (0.5 * GM_CHUNK ** -0.5),
        "gm_bs": 1.0 + 0.1 * n(ks[9], (DEPTH, GM_GROUPS, GM_CHUNK)),
        "out_norm_a": 1.0 + 0.02 * n(ks[10], (DEPTH, ATT_WIDTH)),
        "out_norm_b": 1.0 + 0.02 * n(ks[11], (DEPTH, GM_WIDTH)),
        "w_o": n(ks[12], (DEPTH, D_MIX, D_MODEL)) * (D_MIX ** -0.5) * BETA,
        "ln1_g": 1.0 + 0.02 * n(ks[13], (DEPTH, D_MODEL)),
        "ln1_b": 0.02 * n(ks[14], (DEPTH, D_MODEL)),
        "w_router": n(ks[15], (D_MODEL, N_EXPERTS)) * (D_MODEL ** -0.5),
        "router_bias": 0.01 * n(ks[16], (N_EXPERTS,)),
        "w_gate": n(ks[17], (DEPTH, N_EXPERTS, D_MODEL, D_EXPERT)) * (D_MODEL ** -0.5),
        "w_up": n(ks[18], (DEPTH, N_EXPERTS, D_MODEL, D_EXPERT)) * (D_MODEL ** -0.5) * BETA,
        "w_down": n(ks[19], (DEPTH, N_EXPERTS, D_EXPERT, D_MODEL)) * (D_EXPERT ** -0.5) * BETA,
        "ln2_g": 1.0 + 0.02 * n(ks[20], (DEPTH, D_MODEL)),
        "ln2_b": 0.02 * n(ks[21], (DEPTH, D_MODEL)),
    }

def reference(x_prompt, x_sample, cache_k, cache_v, w_in, sinks, gm_ln_g, gm_ln_b, gm_ws, gm_bs,
              out_norm_a, out_norm_b, w_o, ln1_g, ln1_b, w_router, router_bias,
              w_gate, w_up, w_down, ln2_g, ln2_b):

    def layer_tail(x, l, att_o, gm_o):
        mixed = jnp.concatenate([rms_norm(att_o, out_norm_a[l]), rms_norm(gm_o, out_norm_b[l])], -1)
        x = layer_norm(ALPHA * x + jnp.einsum('bse,ed->bsd', mixed, w_o[l]), ln1_g[l], ln1_b[l])
        y = grouped_moe(x, w_router, router_bias, w_gate[l], w_up[l], w_down[l])
        return layer_norm(ALPHA * x + y, ln2_g[l], ln2_b[l])

    pos_p = jnp.arange(x_prompt.shape[1])
    xp = x_prompt
    kp_new, vp_new = [], []
    for l in range(DEPTH):
        q, k, v, u, gv = split_proj(xp, w_in[l])
        q = rope(q, pos_p)
        k = rope(k, pos_p)
        att_o = window_attention_prompt(q, k, v, sinks[l])
        gm_o = gmlp_prompt(u, gv, gm_ln_g[l], gm_ln_b[l], gm_ws[l], gm_bs[l])
        kp_new.append(k[:, -WINDOW:])
        vp_new.append(v[:, -WINDOW:])
        xp = layer_tail(xp, l, att_o, gm_o)

    pos_s = PAST_LEN + jnp.arange(x_sample.shape[1])
    xs = x_sample
    ks_new, vs_new, gms_new = [], [], []
    for l in range(DEPTH):
        q, k, v, u, gv = split_proj(xs, w_in[l])
        q = rope(q, pos_s)
        k = rope(k, pos_s)
        att_o = window_attention_sample(q, k, v, cache_k[l], cache_v[l], sinks[l])
        gm_o, gm_v = gmlp_sample(u, gv, gm_ln_g[l], gm_ln_b[l], gm_ws[l], gm_bs[l])
        ks_new.append(k)
        vs_new.append(v)
        gms_new.append(gm_v)
        xs = layer_tail(xs, l, att_o, gm_o)

    return (xp, xs, jnp.stack(kp_new), jnp.stack(vp_new), jnp.stack(ks_new), jnp.stack(vs_new), jnp.stack(gms_new))


_drawn_inputs = setup_inputs


def setup_inputs(seed=0):
    import zlib

    import numpy as np

    out = dict(_drawn_inputs(seed))
    spreads = {}
    factors = {'sinks': 8.0, 'gm_ln_g': 7.362, 'gm_ln_b': 7.668, 'out_norm_a': 5.17, 'out_norm_b': 11.878}
    for name, (base, spread) in spreads.items():
        noise = np.random.default_rng([zlib.crc32(name.encode()), seed]).standard_normal(out[name].shape)
        drawn = base * np.exp(spread * noise) if base else spread * noise
        out[name] = __import__('jax').numpy.asarray(drawn.astype(out[name].dtype))
    for name, factor in factors.items():
        out[name] = (out[name] * factor).astype(out[name].dtype)
    return out
```

```python
from contextlib import ExitStack

import numpy as np

import concourse.bass as bass
from concourse import mybir

F32 = mybir.dt.float32
F32R = mybir.dt.float32r
I32 = mybir.dt.int32
U32 = mybir.dt.uint32
ALU = mybir.AluOpType
ACT = mybir.ActivationFunctionType
AX = mybir.AxisListType.X

P = 128
D = 1024
KT_N = D // P
SEQ, DEC, PAST = 512, 64, 256
DEPTH = 2
NT = 5
ROWS = NT * P
HALF = 512
NE = 16
NG = 4
EPG = NE // NG
CAP = ROWS
NSLOT = NE * CAP
BLOCKS = CAP // P
ALPHA = float((2 * DEPTH) ** 0.25)
EPS = 1e-5
BIG = 1e30
SCALE = 64 ** -0.5
OOB = 1 << 20

UNITS_PROJ = 8
UNITS_WO = 4
PAIR_UNITS = 12
PAIRS = NE // 2
UNITS = UNITS_PROJ + UNITS_WO + PAIRS * PAIR_UNITS
RB = 4
SO_MOE = UNITS_PROJ + UNITS_WO
OVB = NE * (BLOCKS - 1)


def fill_plan():
    count = dict.fromkeys("ABCDEFGH", 0)
    at = {}

    def fill(name, bank):
        at[name] = (bank, count[bank], 0)
        count[bank] += 1

    for t in range(NT):
        for h in range(2):
            fill(("xt", t, h), "EF"[h])
    for g in range(4):
        for t in range(NT):
            fill(("proj", g, t), "ABCD"[(g * NT + t) % 4])
    fill("kt0", "E")
    fill("kt1", "F")
    fill("wst", "H")
    for t in range(NT):
        fill(("qt", t), "H")
        for j in range(4):
            fill(("s", t, j), "ABCD"[j])
        fill(("gm", t), "H")
        if t:
            for j in range(4):
                fill(("pt", t - 1, j), "EF"[j % 2])
            fill(("o", t - 1), "G")
    for j in range(4):
        fill(("pt", NT - 1, j), "EF"[j % 2])
    fill(("o", NT - 1), "G")
    for t in range(NT):
        for h in range(2):
            fill(("mt", t, h), "EF"[h])
    for c in range(2):
        for t in range(NT):
            fill(("wo", c, t), "ABCD"[(c * NT + t) % 4])
    for t in range(NT):
        for h in range(2):
            fill(("rt", t, h), "EF"[h])
    fill("logit", "H")
    fill("rank", "H")
    fill("index", "H")
    for s in range(2):
        for h in range(2):
            at["xe", s, h] = ("EF"[h], count["EF"[h]] + s, 2)
        for name, bank in (("gate", "A"), ("up", "B"), ("down0", "C"), ("down1", "D"), ("ht", "G")):
            at[name, s] = (bank, count[bank] + s, 2)
    for bank in "EFABCDG":
        count[bank] += 2 * PAIRS
    return at, count


def build(nc, x_prompt, x_sample, cache_k, cache_v, w_in, sinks, gm_ln_g, gm_ln_b, gm_ws, gm_bs,
          out_norm_a, out_norm_b, w_o, ln1_g, ln1_b, w_router, router_bias, w_gate, w_up, w_down,
          ln2_g, ln2_b, c_rope, c_mask, c_mats, c_ints,
          y_prompt, y_sample, k_prompt, v_prompt, k_sample, v_sample, gmv_sample):
    FILL, NFILL = fill_plan()
    ctx = ExitStack()
    with ctx:
        def sb(name, shape, dt=F32):
            return ctx.enter_context(nc.sbuf_tensor(name, shape, dt))

        def sem(name):
            return ctx.enter_context(nc.semaphore(name))

        def over(base, name, shape, dt=F32, at=0):
            return nc.alloc_sbuf_tensor_at(name, shape, dt, offset=base + at)

        raw = sb("raw", [P, RB, 4, HALF])
        w_hi = sb("w_hi", [P, RB, 4, HALF], F32R)
        w_lo = sb("w_lo", [P, RB, 4, HALF], F32R)
        x = sb("x", [P, NT, D])
        base_t = nc.sbuf_base
        arena_t = sb("arena_t", [P, 2 * KT_N * ROWS])
        base_m = nc.sbuf_base
        arena_m = sb("arena_m", [P, NT * (3 * HALF + 256)])
        table = sb("table", [P, 4, HALF])
        rope = sb("rope", [P, NT, 2, 64])
        mats = sb("mats", [P, 3 * P + 46])
        small = sb("small", [P, 400])
        ints = sb("ints", [P, 2 * NT + NSLOT // P], I32)
        wrt = sb("wrt", [P, KT_N, NE])

        xt_hi = over(base_t, "xt_hi", [P, KT_N, ROWS], F32R)
        xt_lo = over(base_t, "xt_lo", [P, KT_N, ROWS], F32R, 4 * KT_N * ROWS)
        keys_t = over(base_t, "keys_t", [P, 7 * P])
        q_t = over(base_t, "q_t", [P, 2, 4, P], at=3584)
        probs = over(base_t, "probs", [P, 2, 4, 2, 256], at=7680)
        probs_t = over(base_t, "probs_t", [P, 2, 4, P], at=24064)
        cache = over(base_t, "cache", [P, 2, P], at=28160)
        zeros = over(base_t, "zeros", [P, P], at=29184)
        mask = over(base_t, "mask", [P, 3, 256], at=29696)
        ws = over(base_t, "ws", [P, 4, P], at=32768)
        ws_t = over(base_t, "ws_t", [P, 4, P], at=34816)
        squares = over(base_t, "squares", [P, HALF], at=36864)

        QB = 4 * NT * HALF
        q = over(base_m, "q", [P, NT, HALF])
        u = over(base_m, "u", [P, NT, HALF], at=QB)
        gv = over(base_m, "gv", [P, NT, HALF], at=2 * QB)
        kv = over(base_m, "kv", [P, NT, 256], at=3 * QB)
        rope_a = over(base_m, "rope_a", [P, HALF], at=2 * QB)
        rope_b = over(base_m, "rope_b", [P, HALF], at=2 * QB + 4 * HALF)
        x1_t = over(base_m, "x1_t", [P, 2, KT_N, P])
        rows = over(base_m, "rows", [P, 2, D])
        expert_out = over(base_m, "expert_out", [P, 2, D], at=QB)
        act_gate = over(base_m, "act_gate", [P, 2, HALF], at=2 * QB)
        hidden = over(base_m, "hidden", [P, 2, HALF], at=2 * QB + 8 * HALF)
        y_rows = over(base_m, "y_rows", [P, 2, 2, D])

        ident, before, ones = mats[:, 0:P], mats[:, P:2 * P], mats[:, 2 * P:3 * P]
        c0 = 3 * P
        desc16, slot0 = mats[:, c0:c0 + 16], mats[:, c0 + 16:c0 + 32]
        desc4, valid, invalid = mats[:, c0 + 32:c0 + 36], mats[:, c0 + 36:c0 + 41], mats[:, c0 + 41:c0 + 46]
        row_of_value, nowhere = ints[:, 0:2 * NT], ints[:, 2 * NT:2 * NT + NSLOT // P]

        at = [0]

        def sm(*shape):
            n = int(np.prod(shape))
            at[0] += n
            v = small[:, at[0] - n:at[0]]
            if len(shape) == 2:
                return v.rearrange("p (a b) -> p a b", a=shape[0])
            return v

        sink, bs, rbias, eps = sm(8), sm(4), sm(NE), sm(1)
        top, ntop, den, rden = sm(2, 8), sm(2, 8), sm(2, 8), sm(2, 8)
        sink_top, esink = sm(2, 8), sm(2, 8)
        gm_var, gm_sd, gm_rs = sm(4 * NT, 2), sm(4 * NT), sm(4 * NT)
        mv, sd, rs = sm(NT, 2), sm(NT), sm(NT)
        sq, rms, rn = sm(2 * NT), sm(2 * NT), sm(2 * NT)
        w12 = sm(NT, 2)
        shared = sm(4 * NT * 6)
        gm_stats = shared.rearrange("p (a b) -> p a b", b=6)
        stats = shared[:, 0:NT * 12].rearrange("p (t h b) -> p t h b", t=NT, h=2)

        def rcols(k, n, name):
            return over(base_m, name, [P, n], at=3 * QB + 320 * k)

        score, sel, in_group, sel2, pick1, pick2, pick, work, rcol = (
            rcols(k, 80, n) for k, n in enumerate(("score", "sel", "in_group", "sel2", "pick1", "pick2", "pick",
                                                   "work", "rcol")))
        r20 = [over(base_m, f"r20_{k}", [P, NT * NG], at=3 * QB + 2880 + 96 * k) for k in range(10)]
        r5 = [over(base_m, f"r5_{k}", [P, NT], at=3 * QB + 3840 + 32 * k) for k in range(7)]
        idx_rows = over(base_m, "idx_rows", [NE, P], I32, at=3 * QB + 4096)
        idx_f = over(base_m, "idx_f", [NE, P], at=3 * QB + 4608)

        slots = sb("slots", [P, 2 * NT], I32)
        count_max = sb("count_max", [P, 1], I32)
        idx = sb("idx", [P, 2, NE], I32)
        cur_src = sb("cur_src", [P, 2], I32)
        cur_res = sb("cur_res", [P, 2], I32)

        ov_res, ov_src = sb("ov_res", [P, 1], I32), sb("ov_src", [P, 1], I32)

        x1_dram = nc.dram_tensor("x1_rows", [ROWS, D], F32, kind="Internal").ap()
        y2_dram = nc.dram_tensor("y2_rows", [2 * ROWS, D], F32, kind="Internal").ap()
        slot_dram = nc.dram_tensor("slot_rows", [NSLOT, 1], I32, kind="Internal").ap()

        bank = {b: ctx.enter_context(nc.psum_tensor("bank" + b, [P, HALF], F32)) for b in "ABCDEFGH"}

        filled = {b: sem("filled" + b) for b in "ABCDEFGH"}
        freed = {b: sem("freed" + b) for b in "ABCDEFGH"}
        raw_in = [sem(f"raw_in{i}") for i in range(RB)]
        hi_done = sem("hi_done")
        lo_done = sem("lo_done")
        half_used = sem("half_used")
        boot = sem("boot")
        go = sem("go")
        held_pool, held_act, held_dve, held_pe, held_sp = (sem("held_" + n) for n in ("pool", "act", "dve", "pe", "sp"))
        x_ready = sem("x_ready")
        layer_in, att_in = sem("layer_in"), sem("att_in")
        hi_x, hi_m, hi_e, hi_h = sem("hi_x"), sem("hi_m"), sem("hi_e"), sem("hi_h")
        q_done, k_done = sem("q_done"), sem("k_done")
        gm_var_done, gm_sd_done = sem("gm_var_done"), sem("gm_sd_done")
        vn_done = sem("vn_done")
        zero_done, tril_done = sem("zero_done"), sem("tril_done")
        top_done, exp_done = sem("top_done"), sem("exp_done")
        sq_done, norm_done = sem("sq_done"), sem("norm_done")
        kv_out = sem("kv_out")
        table1_in, table2_in = sem("table1_in"), sem("table2_in")
        var1, sd1, var2, sd2 = sem("var1"), sem("sd1"), sem("var2"), sem("sd2")
        x1_ready, x1_out = sem("x1_ready"), sem("x1_out")
        score_done, pick_done, slot_done = sem("score_done"), sem("pick_done"), sem("slot_done")
        slots_init, slots_out, idx_in = sem("slots_init"), sem("slots_out"), sem("idx_in")
        idx_f_done, idx_done, rows_zero = sem("idx_f_done"), sem("idx_done"), sem("rows_zero")
        cur_done = sem("cur_done")
        rows_in = [sem("rows_in0"), sem("rows_in1")]
        out_sent = [sem("out_sent0"), sem("out_sent1")]
        out_free = sem("out_free")
        y_in = [sem("y_in0"), sem("y_in1")]
        y_used = sem("y_used")
        stores = sem("stores")
        ov_pe, ov_act, ov_dve = sem("ov_pe"), sem("ov_act"), sem("ov_dve")
        ov_unit, ov_idx, ov_rows, ov_sent = sem("ov_unit"), sem("ov_idx"), sem("ov_rows"), sem("ov_sent")

        block = ctx.enter_context(nc.Block())

        HALVES = 6 + 4 * PAIRS
        CUR = 4 * PAIRS

        def nth(name, l, i=0):
            b, base, stride = FILL[name]
            return l * NFILL[b] + (i * stride if stride else 0) + (base + 1)

        def wait_filled(eng, name, l, i=0):
            eng.wait_ge(filled[FILL[name][0]], nth(name, l, i))

        def wait_free(eng, name, l, i=0):
            eng.wait_ge(freed[FILL[name][0]], nth(name, l, i))

        def wait_read(eng, name, l, i=0):
            eng.wait_ge(freed[FILL[name][0]], nth(name, l, i) + 1)

        def bank_of(name):
            return bank[FILL[name][0]]

        def done(ins, name):
            ins.then_inc(filled[FILL[name][0]], 1)

        def read(ins, name):
            ins.then_inc(freed[FILL[name][0]], 1)

        def unit_no(l, s, i=0):
            return l * UNITS + s + (i * PAIR_UNITS if s >= SO_MOE else 0)

        def width(s):
            return 256 if s in (2, 3) else HALF

        def wait_slot(act, l, s, i):
            if s < RB:
                act.wait_ge(x_ready, l + 1)
                return
            old = s - RB
            if old < SO_MOE:
                if old % 2 == 0:
                    act.wait_ge(half_used, l * HALVES + (old // 2 + 1))
                else:
                    wait_filled(act, ("proj", old // 2, NT - 1) if old < UNITS_PROJ else ("wo", (old - UNITS_PROJ) // 2, NT - 1), l)
                return
            old -= SO_MOE
            if old >= PAIR_UNITS:
                raise ValueError("units 0 to 3 of a pair are asked for by split_next")
            if old < 8 and old % 2 == 0:
                act.wait_ge(half_used, l * HALVES + i * 4 + (6 + old // 2 + 1))
            elif old < 8:
                wait_filled(act, (("gate", "up")[old // 2 % 2], old // 4), l, i)

        def split_hi(act, l, s, i=0, after=None):
            act.wait_ge(raw_in[s % RB], l * (UNITS // RB * 16) + (i * (PAIR_UNITS // RB * 16) if s >= SO_MOE else 0)
                        + 16 * (s // RB + 1))
            if after is not None:
                wait_filled(act, after, l, i - 1)
            else:
                wait_slot(act, l, s, i)
            n = width(s)
            act.activation(w_hi[:, s % RB, :, 0:n], raw[:, s % RB, :, 0:n], ACT.Copy).then_inc(hi_done, 1)

        def split_lo(dve, l, s, i=0):
            dve.wait_ge(hi_done, unit_no(l, s, i) + 1)
            n = width(s)
            dve.tensor_tensor(w_lo[:, s % RB, :, 0:n], raw[:, s % RB, :, 0:n],
                              w_hi[:, s % RB, :, 0:n].bitcast(F32), ALU.subtract).then_inc(lo_done, 1)

        def wait_unit(pe, l, s, i=0):
            pe.wait_ge(lo_done, unit_no(l, s, i) + 1 + RB)

        def hi_out(act, name, l, dst, s, i=0):
            wait_filled(act, name, l, i)
            act.activation(dst, bank_of(name)[:, :].rearrange("p (k n) -> p k n", k=4), ACT.Copy).then_inc(s, 1)

        def lo_out(dve, name, l, lo, hi, s, value, i=0):
            dve.wait_ge(s, value)
            read(dve.tensor_tensor(lo, bank_of(name)[:, :].rearrange("p (k n) -> p k n", k=4), hi.bitcast(F32),
                                   ALU.subtract), name)

        def t_cols(buf, h, c):
            return buf[:, 4 * h:4 * h + 4, c * P:(c + 1) * P]

        PE_STEPS, ACT_STEPS, DVE_STEPS = 7, 11, 12

        def overflow(eng, l, past, body, apart, close=None):
            eng.wait_ge(slot_done, l + 1)
            eng.sem_inc(apart, 1)
            most = eng.value_load(count_max[0:1, 0:1], min_val=0, max_val=ROWS)
            with eng.If(most > P):
                ran0 = eng.snap(past, min_val=0, max_val=DEPTH * OVB)
                with eng.Fori(0, NE) as e:
                    with eng.Fori(1, BLOCKS) as b:
                        body(e, b, ran0 + e * (BLOCKS - 1) + b - 1)
                if close is not None:
                    close(ran0 + OVB)
                eng.reg_add(past, past, OVB)

        def new_past(eng):
            past = eng.alloc_register("past")
            eng.reg_mov(past, 0)
            return past

        @block.sync
        def _(sp):
            def load(l, s, src, i=0, n=HALF):
                sp.wait_ge(lo_done, unit_no(l, s, i) + 1)
                sp.dma_start(raw[:, s % RB, :, 0:n], src.rearrange("(t p) n -> p t n", p=P)) \
                    .then_inc(raw_in[s % RB], 16)

            for dst, src in ((x[:, 0:4, :], x_prompt[0].rearrange("(t p) d -> p t d", p=P)),
                             (x[0:DEC, 4, :], x_sample[0]),
                             (mats[:, :], c_mats), (ints[:, :], c_ints),
                             (rope[:, :, :, :], c_rope.rearrange("(t p) c n -> p t c n", p=P)),
                             (wrt[:, :, :], w_router.rearrange("(k p) e -> p k e", p=P)),
                             (rbias, router_bias.partition_broadcast(P))):
                sp.dma_start(dst, src).then_inc(boot, 16)

            past = new_past(sp)
            with sp.Fori(0, DEPTH) as l:
                s = 0
                for c0, n in ((0, HALF), (HALF, 256), (1280, HALF), (768, HALF)):
                    for k in range(2):
                        load(l, s, w_in[l, k * HALF:(k + 1) * HALF, c0:c0 + n], n=n)
                        s += 1
                for c in range(2):
                    for k in range(2):
                        load(l, s, w_o[l, k * HALF:(k + 1) * HALF, c * HALF:(c + 1) * HALF])
                        s += 1
                with sp.Fori(0, PAIRS) as i:
                    s = SO_MOE
                    for e in range(2):
                        for w in (w_gate, w_up):
                            for k in range(2):
                                load(l, s, w[l, 2 * i + e, k * HALF:(k + 1) * HALF, :], i)
                                s += 1
                    for e in range(2):
                        for c in range(2):
                            load(l, s, w_down[l, 2 * i + e, :, c * HALF:(c + 1) * HALF], i)
                            s += 1

                def block_units(e, b, ran):
                    srcs = [w[l, e, k * HALF:(k + 1) * HALF, :] for w in (w_gate, w_up) for k in range(2)]
                    srcs += [w_down[l, e, :, c * HALF:(c + 1) * HALF] for c in range(2)]
                    for n, src in enumerate(srcs):
                        sp.wait_ge(ov_dve, ran * DVE_STEPS + (1, 4, 5, 6, 7, 10)[n])
                        sp.dma_start(raw[:, n % RB, :, :], src.rearrange("(t p) n -> p t n", p=P)).then_inc(ov_unit, 16)

                def units_used(ran):
                    sp.wait_ge(ov_unit, ran * (16 * 6))
                    sp.sem_inc(held_sp, 1)
                    sp.wait_ge(ov_dve, ran * DVE_STEPS)
                    sp.sem_inc(held_sp, 1)

                overflow(sp, l, past, block_units, held_sp, units_used)

        @block.gpsimd
        def _(pool):
            def hold(s, v):
                pool.wait_ge(s, v)
                pool.sem_inc(held_pool, 1)

            pool.memset(eps, EPS).then_inc(go, 1)
            pool.sem_inc(out_free, 2)
            past = new_past(pool)
            with pool.Fori(0, DEPTH) as l:
                hold(x_ready, l + 1)
                for dst, src in ((table[:, 0, :], gm_ln_g[l].rearrange("g c -> (g c)").partition_broadcast(P)),
                                 (table[:, 1, :], gm_ln_b[l].rearrange("g c -> (g c)").partition_broadcast(P)),
                                 (table[:, 2, :], out_norm_a[l].partition_broadcast(P)),
                                 (table[:, 3, :], out_norm_b[l].partition_broadcast(P)),
                                 (sink, sinks[l].partition_broadcast(P))):
                    pool.dma_start(dst, src).then_inc(layer_in, 16)
                pool.dma_start(bs, gm_bs[l].rearrange("g p -> p g"), allow_slow_non_contiguous=True).then_inc(layer_in, 16)
                pool.dma_start(slot_dram.rearrange("(p n) o -> p (n o)", p=P), nowhere).then_inc(slots_init, 16)
                hold(filled[FILL["proj", 3, NT - 1][0]], nth(("proj", 3, NT - 1), l))
                for dst, src in ((mask[:, :, :], c_mask.rearrange("c p n -> p c n")),
                                 (cache[:, 0, :], cache_k[l, 0].rearrange("s h d -> s (h d)")),
                                 (cache[:, 1, :], cache_v[l, 0].rearrange("s h d -> s (h d)")),
                                 (ws[:, :, :], gm_ws[l].rearrange("g p q -> p g q"))):
                    pool.dma_start(dst, src).then_inc(att_in, 16)
                pool.memset(zeros[:, :], 0.0).then_inc(zero_done, 1)
                pool.memset(keys_t[:, 0:P], 0.0).then_inc(zero_done, 1)
                hold(att_in, 64 * l + 64)
                pool.affine_select(out=ws[:, :, :], in_=ws[:, :, :], compare_op=ALU.is_ge, fill=0.0, base=0,
                                   pattern=[[0, 4], [-1, P]], channel_multiplier=1).then_inc(tril_done, 1)
                hold(k_done, NT * l + NT)
                for dst, src in ((k_prompt[l, 0], kv[:, 3, 0:P]), (v_prompt[l, 0], kv[:, 3, P:256]),
                                 (k_sample[l, 0], kv[0:DEC, 4, 0:P]), (v_sample[l, 0], kv[0:DEC, 4, P:256])):
                    pool.dma_start(dst.rearrange("s h d -> s (h d)"), src).then_inc(kv_out, 16)
                hold(vn_done, NT * l + NT)
                pool.dma_start(gmv_sample[l, 0], gv[0:DEC, 4, :]).then_inc(kv_out, 16)
                hold(norm_done, 2 * NT * l + 2 * NT)
                pool.dma_start(table[:, 0:2, :], ln1_g[l].rearrange("(a c) -> a c", a=2).partition_broadcast(P)).then_inc(table1_in, 16)
                pool.dma_start(table[:, 2:4, :], ln1_b[l].rearrange("(a c) -> a c", a=2).partition_broadcast(P)).then_inc(table1_in, 16)
                for t in range(NT):
                    hold(x1_ready, NT * l + t + 1)
                    pool.dma_start(x1_dram[t * P:(t + 1) * P, :], x[:, t, :]).then_inc(x1_out, 16)
                pool.dma_start(table[:, 0:2, :], ln2_g[l].rearrange("(a c) -> a c", a=2).partition_broadcast(P)).then_inc(table2_in, 16)
                pool.dma_start(table[:, 2:4, :], ln2_b[l].rearrange("(a c) -> a c", a=2).partition_broadcast(P)).then_inc(table2_in, 16)
                hold(slots_init, 16 * l + 16)
                hold(slot_done, l + 1)
                for c in range(2 * NT):
                    pool.indirect_dma_start(
                        out=slot_dram, out_offset=bass.IndirectOffsetOnAxis(ap=slots[:, c:c + 1].bitcast(U32), axis=0),
                        in_=row_of_value[:, c:c + 1], in_offset=None, bounds_check=NSLOT - 1, oob_is_err=False) \
                        .then_inc(slots_out, 16)
                hold(slots_out, 16 * 2 * NT * (l + 1))
                pool.dma_start(idx_rows[:, :], slot_dram.rearrange("(e s) o -> e (s o)", e=NE)[:, 0:P]).then_inc(idx_in, 16)
                hold(x1_out, 16 * NT * (l + 1))
                hold(idx_done, l + 1)
                hold(rows_zero, l + 1)

                def gather(s):
                    pool.indirect_dma_start(
                        out=rows[:, s, :], out_offset=None, in_=x1_dram,
                        in_offset=bass.IndirectOffsetOnAxis(ap=cur_src[:, s:s + 1].bitcast(U32), axis=0),
                        bounds_check=ROWS - 1, oob_is_err=False).then_inc(rows_in[s], 16)

                def scatter(s):
                    pool.indirect_dma_start(
                        out=y2_dram, out_offset=bass.IndirectOffsetOnAxis(ap=cur_res[:, s:s + 1].bitcast(U32), axis=0),
                        in_=expert_out[:, s, :], in_offset=None,
                        bounds_check=2 * ROWS - 1, oob_is_err=False).then_inc(out_sent[s], 16)

                for s in range(2):
                    pool.tensor_copy(cur_src[:, s:s + 1], idx[:, 1, s:s + 1]).then_inc(cur_done, 1)
                hold(cur_done, l * CUR + 2)
                for s in range(2):
                    gather(s)

                def pair(i, last=False):
                    n0 = l * CUR + i * 4 + 2
                    if not last:
                        for s in range(2):
                            hold(filled["F"], nth(("xe", s, 1), l, i))
                            hold(rows_in[s], 16 * (l * PAIRS + i + 1))
                            pool.tensor_copy(cur_src[:, s:s + 1], idx[:, 1, bass.ds(2 * i + 2 + s, 1)]).then_inc(cur_done, 1)
                        hold(cur_done, n0 + 2)
                        for s in range(2):
                            gather(s)
                    for s in range(2):
                        pool.tensor_copy(cur_res[:, s:s + 1], idx[:, 0, bass.ds(2 * i + s, 1)]).then_inc(cur_done, 1)
                    hold(cur_done, n0 + (2 if last else 4))
                    for s in range(2):
                        for c in range(2):
                            hold(freed["CD"[c]], nth((f"down{c}", s), l, i) + 1)
                        scatter(s)
                    for s in range(2):
                        hold(out_sent[s], 16 * (l * PAIRS + i + 1))
                        pool.sem_inc(out_free, 1)

                with pool.Fori(0, PAIRS - 1) as i:
                    pair(i)
                pair(PAIRS - 1, last=True)

                def block_rows(e, b, ran):
                    pool.dma_start(ov_res[:, :], slot_dram[bass.ds(e * CAP + b * P, P), :]).then_inc(ov_idx, 16)
                    hold(ov_dve, ran * DVE_STEPS + 1)
                    pool.indirect_dma_start(
                        out=rows[:, 0, :], out_offset=None, in_=x1_dram,
                        in_offset=bass.IndirectOffsetOnAxis(ap=ov_src[:, 0:1].bitcast(U32), axis=0),
                        bounds_check=ROWS - 1, oob_is_err=False).then_inc(ov_rows, 16)
                    hold(ov_act, ran * ACT_STEPS + 11)
                    hold(ov_dve, ran * DVE_STEPS + 12)
                    pool.indirect_dma_start(
                        out=y2_dram, out_offset=bass.IndirectOffsetOnAxis(ap=ov_res[:, 0:1].bitcast(U32), axis=0),
                        in_=expert_out[:, 0, :], in_offset=None,
                        bounds_check=2 * ROWS - 1, oob_is_err=False).then_inc(ov_sent, 16)
                    hold(ov_sent, 16 * (ran + 1))

                overflow(pool, l, past, block_rows, held_pool)

            hold(x_ready, DEPTH + 1)
            pool.dma_start(y_prompt[0].rearrange("(t p) d -> p t d", p=P), x[:, 0:4, :]).then_inc(stores, 16)
            pool.dma_start(y_sample[0], x[0:DEC, 4, :]).then_inc(stores, 16)
            pool.wait_ge(stores, 32)
            pool.wait_ge(kv_out, 16 * 5 * DEPTH)

        @block.scalar
        def _(act):
            act.wait_ge(boot, 16 * 7)
            act.wait_ge(go, 1)
            past = new_past(act)
            with act.Fori(0, DEPTH) as l:
                for t in range(NT):
                    for h in range(2):
                        hi_out(act, ("xt", t, h), l, t_cols(xt_hi, h, t), hi_x)
                    if t == 0:
                        split_hi(act, l, 0)
                        split_hi(act, l, 1)
                for s in (2, 3, 4, 5, 6, 7):
                    split_hi(act, l, s)
                for g, dst, units in ((2, gv, (8, 9)), (3, u, (10, 11))):
                    for t in range(NT):
                        if t == 0:
                            act.wait_ge(k_done, NT * l + NT)
                        wait_filled(act, ("proj", g, t), l)
                        read(act.activation(dst[:, t, :], bank_of(("proj", g, t))[:, :], ACT.Gelu), ("proj", g, t))
                    if g == 2:
                        for s in units:
                            split_hi(act, l, s)
                act.wait_ge(gm_var_done, l + 1)
                act.activation(gm_sd, gm_var[:, :, 1], ACT.Sqrt, bias=eps).then_inc(gm_sd_done, 1)
                for s in (10, 11):
                    split_hi(act, l, s)
                wait_filled(act, "kt0", l)
                read(act.activation(keys_t[:, P:5 * P], bank_of("kt0")[:, :], ACT.Copy), "kt0")
                wait_filled(act, "kt1", l)
                read(act.activation(keys_t[:, 5 * P:7 * P], bank_of("kt1")[:, 0:2 * P], ACT.Copy), "kt1")
                wait_filled(act, "wst", l)
                read(act.activation(ws_t[:, :, :], bank_of("wst")[:, :].rearrange("p (g n) -> p g n", g=4), ACT.Copy), "wst")

                def probs_out(t):
                    for j in range(4):
                        wait_filled(act, ("pt", t, j), l)
                        read(act.activation(probs_t[:, j % 2, :, :], bank_of(("pt", t, j))[:, :].rearrange("p (a n) -> p a n", a=4),
                                            ACT.Copy), ("pt", t, j))

                for t in range(NT):
                    wait_filled(act, ("qt", t), l)
                    read(act.activation(q_t[:, t % 2, :, :], bank_of(("qt", t))[:, :].rearrange("p (a n) -> p a n", a=4), ACT.Copy), ("qt", t))
                    if t:
                        probs_out(t - 1)
                    act.wait_ge(top_done, NT * l + t + 1)
                    for h in range(8):
                        act.activation(probs[:, t % 2, h // 2, h % 2, :], probs[:, t % 2, h // 2, h % 2, :], ACT.Exp,
                                       bias=ntop[:, t % 2, h:h + 1], accum_out=den[:, t % 2, h:h + 1]).then_inc(exp_done, 1)
                    act.activation(esink[:, t % 2, :], sink_top[:, t % 2, :], ACT.Exp).then_inc(exp_done, 1)
                probs_out(NT - 1)
                for t in range(NT):
                    wait_read(act, ("o", t), l)
                    act.activation(squares[:, :], q[:, t, :], ACT.Square, accum_out=sq[:, t:t + 1])
                    wait_read(act, ("gm", t), l)
                    act.sem_inc(held_act, 1)
                    act.drain()
                    act.activation(squares[:, :], u[:, t, :], ACT.Square, accum_out=sq[:, NT + t:NT + t + 1])
                    act.drain()
                act.activation(rms, sq, ACT.Sqrt, bias=eps, scale=1.0 / HALF).then_inc(sq_done, 1)
                for t in range(NT):
                    for h in range(2):
                        hi_out(act, ("mt", t, h), l, t_cols(xt_hi, h, t), hi_m)
                for s in (12, 13, 14, 15):
                    split_hi(act, l, s)
                act.wait_ge(var1, l + 1)
                act.activation(sd, mv[:, :, 1], ACT.Sqrt, bias=eps).then_inc(sd1, 1)
                for t in range(NT):
                    for h in range(2):
                        wait_filled(act, ("rt", t, h), l)
                        read(act.activation(x1_t[:, t % 2, 4 * h:4 * h + 4, :],
                                            bank_of(("rt", t, h))[:, :].rearrange("p (a n) -> p a n", a=4), ACT.Copy), ("rt", t, h))
                wait_filled(act, "logit", l)
                act.wait_ge(kv_out, 80 * l + 80)
                read(act.activation(score[:, :], bank_of("logit")[:, 0:NT * NE], ACT.Sigmoid), "logit")

                def rows_hi(i, s):
                    for h in range(2):
                        hi_out(act, ("xe", s, h), l, t_cols(xt_hi, h, s), hi_e, i)

                def gate(i, s):
                    wait_filled(act, ("gate", s), l, i)
                    read(act.activation(act_gate[:, s, :], bank_of(("gate", s))[:, :], ACT.Silu), ("gate", s))

                def hidden_hi(i, s):
                    hi_out(act, ("ht", s), l, xt_hi[:, 0:4, (2 + s) * P:(3 + s) * P], hi_h, i)

                def out0(i, s):
                    wait_filled(act, ("down0", s), l, i)
                    act.wait_ge(out_free, l * NE + 2 * i + (s + 1))
                    read(act.activation(expert_out[:, s, 0:HALF], bank_of(("down0", s))[:, :], ACT.Copy), ("down0", s))

                rows_hi(0, 0)
                rows_hi(0, 1)

                def pair(i, last=False):
                    c = SO_MOE
                    split_hi(act, l, c + 4, i)
                    split_hi(act, l, c + 5, i)
                    gate(i, 0)
                    split_hi(act, l, c + 6, i)
                    split_hi(act, l, c + 7, i)
                    split_hi(act, l, c + 8, i)
                    split_hi(act, l, c + 9, i)
                    hidden_hi(i, 0)
                    gate(i, 1)
                    split_hi(act, l, c + 10, i)
                    split_hi(act, l, c + 11, i)
                    if not last:
                        rows_hi(i + 1, 0)
                        split_hi(act, l, c, i + 1, after=("down0", 0))
                    out0(i, 0)
                    hidden_hi(i, 1)
                    if not last:
                        rows_hi(i + 1, 1)
                        split_hi(act, l, c + 1, i + 1, after=("down1", 0))
                        split_hi(act, l, c + 2, i + 1, after=("down0", 1))
                    out0(i, 1)
                    if not last:
                        split_hi(act, l, c + 3, i + 1, after=("down1", 1))

                with act.Fori(0, PAIRS - 1) as i:
                    pair(i)
                pair(PAIRS - 1, last=True)

                def block_act(e, b, ran):
                    def hi(dst, src, after):
                        act.wait_ge(ov_pe, ran * PE_STEPS + after)
                        act.activation(dst, src, ACT.Copy).then_inc(ov_act, 1)

                    def unit_hi(n):
                        act.wait_ge(ov_unit, 16 * (ran * 6 + n + 1))
                        act.activation(w_hi[:, n % RB, :, :], raw[:, n % RB, :, :], ACT.Copy).then_inc(ov_act, 1)

                    for h in range(2):
                        hi(t_cols(xt_hi, h, 0), bank["EF"[h]][:, :].rearrange("p (k n) -> p k n", k=4), 1 + h)
                    for n in range(4):
                        unit_hi(n)
                    act.wait_ge(ov_pe, ran * PE_STEPS + 3)
                    act.activation(act_gate[:, 0, :], bank["A"][:, :], ACT.Silu).then_inc(ov_act, 1)
                    hi(xt_hi[:, 0:4, 2 * P:3 * P], bank["G"][:, :].rearrange("p (k n) -> p k n", k=4), 5)
                    for n in (4, 5):
                        unit_hi(n)
                    act.wait_ge(ov_pe, ran * PE_STEPS + 6)
                    act.activation(expert_out[:, 0, 0:HALF], bank["C"][:, :], ACT.Copy).then_inc(ov_act, 1)
                    act.wait_ge(ov_sent, 16 * (ran + 1))

                overflow(act, l, past, block_act, held_act)
                act.wait_ge(out_free, NE * (l + 1) + 2)
                for t in range(NT):
                    n = P if t < 4 else DEC
                    if t >= 2:
                        act.wait_ge(y_used, NT * l + t - 1)
                    act.dma_start(y_rows[0:n, t % 2, :, :],
                                  y2_dram[2 * P * t:2 * P * t + 2 * n, :].rearrange("(p j) n -> p j n", j=2)).then_inc(y_in[t % 2], 16)
                act.wait_ge(var2, l + 1)
                act.activation(sd, mv[:, :, 1], ACT.Sqrt, bias=eps).then_inc(sd2, 1)

        @block.vector
        def _(dve):
            dve.sem_inc(lo_done, RB)
            dve.wait_ge(boot, 16 * 7)
            dve.memset(x[DEC:P, 4, :], 0.0).then_inc(x_ready, 1)
            past = new_past(dve)

            def heads(ap, n):
                return ap.rearrange("p (h c d) -> p h c d", h=n, c=2)

            def rotate(psum, n, t, dst, name):
                w = n * 64
                cos = rope[:, t, 0, :].unsqueeze(1).to_broadcast([P, n, 64])
                sin = rope[:, t, 1, :].rearrange("p (c d) -> p c d", c=2)
                a, b = rope_a[:, 0:w], rope_b[:, 0:w]
                dve.tensor_tensor(a.rearrange("p (h d) -> p h d", h=n), psum.rearrange("p (h d) -> p h d", h=n), cos, ALU.mult)
                src, dst4 = heads(psum, n), heads(b, n)
                dve.tensor_tensor(dst4[:, :, 0, :], src[:, :, 1, :], sin[:, 0, :].unsqueeze(1).to_broadcast([P, n, 32]), ALU.mult)
                last = dve.tensor_tensor(dst4[:, :, 1, :], src[:, :, 0, :], sin[:, 1, :].unsqueeze(1).to_broadcast([P, n, 32]), ALU.mult)
                if name is not None:
                    read(last, name)
                dve.drain()
                if n == 8:
                    a, b = (v.rearrange("p (a j d) -> p a j d", a=2, j=4) for v in (a, b))
                    dst = dst.rearrange("p (j a d) -> p a j d", a=2, j=4)
                return dve.tensor_tensor(dst, a, b, ALU.add)

            def layer_norm(t):
                dve.tensor_scalar(x[:, t, :], x[:, t, :], mv[:, t, 0:1], rs[:, t:t + 1], ALU.subtract, ALU.mult)
                dve.drain()
                xt = x[:, t, :].rearrange("p (a c) -> p a c", a=2)
                dve.tensor_tensor(xt, xt, table[:, 0:2, :], ALU.mult)
                dve.drain()
                return dve.tensor_tensor(xt, xt, table[:, 2:4, :], ALU.add)

            def row_stats(t):
                for h in range(2):
                    dve.bn_stats(stats[:, t, h, :], x[:, t, h * HALF:(h + 1) * HALF])

            def lo_rows(l, name, h, c, s, value, i=0):
                lo_out(dve, name, l, t_cols(xt_lo, h, c), t_cols(xt_hi, h, c), s, value, i)

            with dve.Fori(0, DEPTH) as l:
                for t in range(NT):
                    for h in range(2):
                        lo_rows(l, ("xt", t, h), h, t, hi_x, 2 * NT * l + (2 * t + h + 1))
                    if t == 0:
                        split_lo(dve, l, 0)
                        split_lo(dve, l, 1)
                split_lo(dve, l, 2)
                split_lo(dve, l, 3)
                for t in range(NT):
                    name = ("proj", 0, t)
                    wait_filled(dve, name, l)
                    rotate(bank_of(name)[:, :], 8, t, q[:, t, :], name).then_inc(q_done, 1)
                    dve.drain()
                split_lo(dve, l, 4)
                split_lo(dve, l, 5)
                for t in range(NT):
                    name = ("proj", 1, t)
                    wait_filled(dve, name, l)
                    dve.tensor_copy(kv[:, t, P:256], bank_of(name)[:, P:256])
                    rotate(bank_of(name)[:, 0:P], 2, t, kv[:, t, 0:P], name).then_inc(k_done, 1)
                    dve.drain()
                split_lo(dve, l, 6)
                split_lo(dve, l, 7)
                for t in range(NT):
                    wait_read(dve, ("proj", 2, t), l)
                    for g in range(4):
                        dve.bn_stats(gm_stats[:, 4 * t + g, :], gv[:, t, g * P:(g + 1) * P])
                dve.drain()
                for c in range(4 * NT):
                    ins = dve.bn_aggr(gm_var[:, c, :], gm_stats[:, c, :])
                ins.then_inc(gm_var_done, 1)
                split_lo(dve, l, 8)
                split_lo(dve, l, 9)
                dve.wait_ge(gm_sd_done, l + 1)
                dve.reciprocal(gm_rs, gm_sd)
                dve.drain()
                for t in range(NT):
                    for g in range(4):
                        c = 4 * t + g
                        part = gv[:, t, g * P:(g + 1) * P]
                        dve.tensor_scalar(part, part, gm_var[:, c, 0:1], gm_rs[:, c:c + 1], ALU.subtract, ALU.mult)
                dve.wait_ge(layer_in, 96 * l + 96)
                dve.sem_inc(held_dve, 1)
                dve.drain()
                for t in range(NT):
                    dve.tensor_tensor(gv[:, t, :], gv[:, t, :], table[:, 0, :], ALU.mult)
                dve.drain()
                for t in range(NT):
                    dve.tensor_tensor(gv[:, t, :], gv[:, t, :], table[:, 1, :], ALU.add).then_inc(vn_done, 1)
                split_lo(dve, l, 10)
                split_lo(dve, l, 11)

                def attention_out(t):
                    dve.wait_ge(exp_done, 9 * NT * l + 9 * (t + 1))
                    dve.tensor_tensor(den[:, t % 2, :], den[:, t % 2, :], esink[:, t % 2, :], ALU.add)
                    dve.drain()
                    dve.reciprocal(rden[:, t % 2, :], den[:, t % 2, :])
                    dve.drain()
                    wait_filled(dve, ("o", t), l)
                    read(dve.tensor_tensor(q[:, t, :].rearrange("p (h d) -> p h d", h=8),
                                           bank_of(("o", t))[:, :].rearrange("p (h d) -> p h d", h=8),
                                           rden[:, t % 2, :].unsqueeze(2).to_broadcast([P, 8, 64]), ALU.mult), ("o", t))

                dve.wait_ge(att_in, 64 * l + 64)
                for t in range(NT):
                    m = 1 if t == 0 else 2 if t == NT - 1 else 0
                    if t >= 2:
                        wait_filled(dve, ("pt", t - 2, 3), l)
                    for j in range(4):
                        name = ("s", t, j)
                        wait_filled(dve, name, l)
                        read(dve.scalar_tensor_tensor(
                            out=probs[:, t % 2, (0, 2, 1, 3)[j], :, :], in0=bank_of(name)[:, :].rearrange("p (a n) -> p a n", a=2),
                            scalar=SCALE, in1=mask[:, m, :].unsqueeze(1).to_broadcast([P, 2, 256]),
                            op0=ALU.mult, op1=ALU.add), name)
                    dve.drain()
                    dve.tensor_reduce(top[:, t % 2, :], probs[:, t % 2, :, :, :].rearrange("p j a n -> p (j a) n"), AX, ALU.max)
                    dve.drain()
                    dve.tensor_tensor(top[:, t % 2, :], top[:, t % 2, :], sink, ALU.max)
                    dve.drain()
                    dve.tensor_scalar(ntop[:, t % 2, :], top[:, t % 2, :], -1.0, None, ALU.mult)
                    dve.tensor_tensor(sink_top[:, t % 2, :], sink, top[:, t % 2, :], ALU.subtract).then_inc(top_done, 1)
                    name = ("gm", t)
                    wait_filled(dve, name, l)
                    wait_read(dve, ("proj", 3, t), l)
                    for g in range(4):
                        part = u[:, t, g * P:(g + 1) * P]
                        ins = dve.scalar_tensor_tensor(out=part, in0=bank_of(name)[:, g * P:(g + 1) * P], scalar=bs[:, g:g + 1],
                                                       in1=part, op0=ALU.add, op1=ALU.mult)
                    read(ins, name)
                    if t:
                        attention_out(t - 1)
                attention_out(NT - 1)
                dve.wait_ge(sq_done, l + 1)
                dve.reciprocal(rn, rms)
                dve.drain()
                for t in range(NT):
                    for b, v in enumerate((q, u)):
                        dve.scalar_tensor_tensor(out=v[:, t, :], in0=v[:, t, :], scalar=rn[:, b * NT + t:b * NT + t + 1],
                                                 in1=table[:, 2 + b, :], op0=ALU.mult, op1=ALU.mult).then_inc(norm_done, 1)
                for t in range(NT):
                    for h in range(2):
                        lo_rows(l, ("mt", t, h), h, t, hi_m, 2 * NT * l + (2 * t + h + 1))
                for c in range(2):
                    for t in range(NT):
                        name = ("wo", c, t)
                        wait_filled(dve, name, l)
                        part = x[:, t, c * HALF:(c + 1) * HALF]
                        read(dve.scalar_tensor_tensor(out=part, in0=part, scalar=ALPHA, in1=bank_of(name)[:, :],
                                                      op0=ALU.mult, op1=ALU.add), name)
                    if c == 0:
                        split_lo(dve, l, 12)
                        split_lo(dve, l, 13)
                dve.drain()
                for t in range(NT):
                    row_stats(t)
                dve.drain()
                for t in range(NT):
                    ins = dve.bn_aggr(mv[:, t, :], stats[:, t, :, :])
                ins.then_inc(var1, 1)
                split_lo(dve, l, 14)
                split_lo(dve, l, 15)
                dve.wait_ge(sd1, l + 1)
                dve.reciprocal(rs, sd)
                dve.drain()
                dve.wait_ge(table1_in, 32 * l + 32)
                for t in range(NT):
                    layer_norm(t).then_inc(x1_ready, 1)

                wait_read(dve, "logit", l)
                sel3 = sel[:, :].rearrange("p (t e) -> p t e", t=NT)
                score3 = score[:, :].rearrange("p (t e) -> p t e", t=NT)
                dve.tensor_tensor(sel3, score3, rbias.unsqueeze(1).to_broadcast([P, NT, NE]), ALU.add)
                dve.drain()
                s4 = sel[:, :].rearrange("p (a b) -> p a b", b=EPG)
                hi01, lo01, hi23, lo23, best, mid, low, second, group, g_eq = (r[:, :] for r in r20)
                dve.tensor_tensor(hi01, s4[:, :, 0], s4[:, :, 1], ALU.max)
                dve.tensor_tensor(lo01, s4[:, :, 0], s4[:, :, 1], ALU.min)
                dve.tensor_tensor(hi23, s4[:, :, 2], s4[:, :, 3], ALU.max)
                dve.tensor_tensor(lo23, s4[:, :, 2], s4[:, :, 3], ALU.min)
                dve.drain()
                dve.tensor_tensor(best, hi01, hi23, ALU.max)
                dve.tensor_tensor(mid, hi01, hi23, ALU.min)
                dve.tensor_tensor(low, lo01, lo23, ALU.max)
                dve.drain()
                dve.tensor_tensor(second, mid, low, ALU.max)
                dve.drain()
                dve.tensor_tensor(group, best, second, ALU.add)
                dve.drain()

                def first_max(dst, src, n, order, tmp, m):
                    s3, d3, t3 = (v.rearrange("p (a b) -> p a b", b=n) for v in (src, dst, tmp))
                    dve.tensor_reduce(m, s3, AX, ALU.max)
                    dve.drain()
                    dve.tensor_tensor(t3, s3, m.unsqueeze(2).to_broadcast([P, NT, n]), ALU.is_equal)
                    dve.drain()
                    dve.tensor_tensor(t3, t3, order.unsqueeze(1).to_broadcast([P, NT, n]), ALU.mult)
                    dve.drain()
                    dve.tensor_reduce(m, t3, AX, ALU.max)
                    dve.drain()
                    dve.tensor_tensor(d3, t3, m.unsqueeze(2).to_broadcast([P, NT, n]), ALU.is_equal)
                    dve.drain()

                ma, s1, s2, ssum, srec, sl1, sl2 = (r[:, :] for r in r5[0:7])
                first_max(best, group, NG, desc4, g_eq, ma)
                dve.tensor_scalar(low, best, BIG, -BIG, ALU.mult, ALU.add)
                ing = in_group[:, :].rearrange("p (a b) -> p a b", b=EPG)
                dve.tensor_tensor(ing, s4, best.unsqueeze(2).to_broadcast([P, NT * NG, EPG]), ALU.mult)
                dve.drain()
                dve.tensor_tensor(ing, ing, low.unsqueeze(2).to_broadcast([P, NT * NG, EPG]), ALU.add)
                dve.drain()
                first_max(pick1[:, :], in_group[:, :], NE, desc16, work[:, :], ma)
                dve.scalar_tensor_tensor(out=sel2[:, :], in0=pick1[:, :], scalar=-3 * BIG, in1=in_group[:, :], op0=ALU.mult, op1=ALU.add)
                dve.drain()
                first_max(pick2[:, :], sel2[:, :], NE, desc16, work[:, :], ma)
                ok = valid.unsqueeze(2).to_broadcast([P, NT, NE])
                for v in (pick1, pick2):
                    v3 = v[:, :].rearrange("p (t e) -> p t e", t=NT)
                    dve.tensor_tensor(v3, v3, ok, ALU.mult)
                dve.drain()
                dve.tensor_tensor(pick[:, :], pick1[:, :], pick2[:, :], ALU.add).then_inc(pick_done, 1)

                def picked(dst, src, v):
                    dve.tensor_tensor(work[:, :], src, v[:, :], ALU.mult)
                    dve.drain()
                    dve.tensor_reduce(dst, work[:, :].rearrange("p (t e) -> p t e", t=NT), AX, ALU.add)
                    dve.drain()

                picked(s1, score[:, :], pick1)
                picked(s2, score[:, :], pick2)
                dve.tensor_tensor(ssum, s1, s2, ALU.add)
                dve.drain()
                dve.tensor_tensor(ssum, ssum, invalid, ALU.add)
                dve.drain()
                dve.reciprocal(srec, ssum)
                dve.drain()
                dve.tensor_tensor(w12[:, :, 0], s1, srec, ALU.mult)
                dve.tensor_tensor(w12[:, :, 1], s2, srec, ALU.mult)
                wait_filled(dve, "rank", l)
                dve.tensor_tensor(rcol[:, :].rearrange("p (t e) -> p t e", t=NT),
                                  bank_of("rank")[:, 0:NT * NE].rearrange("p (t e) -> p t e", t=NT),
                                  slot0.unsqueeze(1).to_broadcast([P, NT, NE]), ALU.add)
                dve.tensor_reduce(ma[:, 0:1], bank_of("rank")[:, NT * NE:(NT + 1) * NE], AX, ALU.max)
                dve.drain()
                read(dve.tensor_copy(count_max[:, :], ma[:, 0:1]), "rank")
                picked(sl1, rcol[:, :], pick1)
                picked(sl2, rcol[:, :], pick2)
                far = float(OOB)
                slots3 = slots[:, :].rearrange("p (t j) -> p t j", j=2)
                dve.scalar_tensor_tensor(out=slots3[:, :, 0], in0=invalid, scalar=far, in1=sl1, op0=ALU.mult, op1=ALU.add)
                dve.scalar_tensor_tensor(out=slots3[:, :, 1], in0=invalid, scalar=far, in1=sl2, op0=ALU.mult, op1=ALU.add).then_inc(slot_done, 1)
                dve.memset(rows[:, :, :], 0.0).then_inc(rows_zero, 1)
                dve.wait_ge(idx_in, 16 * l + 16)
                dve.tensor_copy(idx_f[:, :], idx_rows[:, :]).then_inc(idx_f_done, 1)
                wait_filled(dve, "index", l)
                read(dve.tensor_copy(idx[:, 0, :], bank_of("index")[:, 0:NE]), "index")
                dve.drain()
                dve.tensor_scalar(idx[:, 1, :], idx[:, 0, :], 1, None, ALU.logical_shift_right).then_inc(idx_done, 1)

                def rows_lo(i, s):
                    for h in range(2):
                        lo_rows(l, ("xe", s, h), h, s, hi_e, 4 * PAIRS * l + 4 * i + (2 * s + h + 1), i)

                def hidden_out(i, s):
                    wait_read(dve, ("gate", s), l, i)
                    wait_filled(dve, ("up", s), l, i)
                    read(dve.tensor_tensor(hidden[:, s, :], act_gate[:, s, :], bank_of(("up", s))[:, :], ALU.mult), ("up", s))

                def hidden_lo(i, s):
                    lo_out(dve, ("ht", s), l, xt_lo[:, 0:4, (2 + s) * P:(3 + s) * P], xt_hi[:, 0:4, (2 + s) * P:(3 + s) * P],
                           hi_h, 2 * PAIRS * l + 2 * i + (s + 1), i)

                def out1(i, s):
                    dve.wait_ge(out_free, l * NE + 2 * i + (s + 1))
                    wait_filled(dve, ("down1", s), l, i)
                    read(dve.tensor_copy(expert_out[:, s, HALF:D], bank_of(("down1", s))[:, :]), ("down1", s))

                rows_lo(0, 0)
                rows_lo(0, 1)

                def pair(i, last=False):
                    c = SO_MOE
                    split_lo(dve, l, c + 4, i)
                    split_lo(dve, l, c + 5, i)
                    hidden_out(i, 0)
                    split_lo(dve, l, c + 6, i)
                    split_lo(dve, l, c + 7, i)
                    split_lo(dve, l, c + 8, i)
                    split_lo(dve, l, c + 9, i)
                    hidden_lo(i, 0)
                    hidden_out(i, 1)
                    split_lo(dve, l, c + 10, i)
                    split_lo(dve, l, c + 11, i)
                    if not last:
                        rows_lo(i + 1, 0)
                        split_lo(dve, l, c, i + 1)
                    out1(i, 0)
                    hidden_lo(i, 1)
                    if not last:
                        rows_lo(i + 1, 1)
                        split_lo(dve, l, c + 1, i + 1)
                        split_lo(dve, l, c + 2, i + 1)
                    out1(i, 1)
                    if not last:
                        split_lo(dve, l, c + 3, i + 1)

                with dve.Fori(0, PAIRS - 1) as i:
                    pair(i)
                pair(PAIRS - 1, last=True)

                def block_dve(e, b, ran):
                    def lo(dst, src, hi, after):
                        dve.wait_ge(ov_act, ran * ACT_STEPS + after)
                        dve.tensor_tensor(dst, src, hi.bitcast(F32), ALU.subtract).then_inc(ov_dve, 1)

                    def unit_lo(n, after):
                        lo(w_lo[:, n % RB, :, :], raw[:, n % RB, :, :], w_hi[:, n % RB, :, :], after)

                    dve.wait_ge(ov_idx, 16 * (ran + 1))
                    dve.tensor_scalar(ov_src[:, :], ov_res[:, :], 1, None, ALU.logical_shift_right).then_inc(ov_dve, 1)
                    for h in range(2):
                        lo(t_cols(xt_lo, h, 0), bank["EF"[h]][:, :].rearrange("p (k n) -> p k n", k=4), t_cols(xt_hi, h, 0), 1 + h)
                    for n in range(4):
                        unit_lo(n, 3 + n)
                    dve.wait_ge(ov_act, ran * ACT_STEPS + 7)
                    dve.wait_ge(ov_pe, ran * PE_STEPS + 4)
                    dve.tensor_tensor(hidden[:, 0, :], act_gate[:, 0, :], bank["B"][:, :], ALU.mult).then_inc(ov_dve, 1)
                    lo(xt_lo[:, 0:4, 2 * P:3 * P], bank["G"][:, :].rearrange("p (k n) -> p k n", k=4), xt_hi[:, 0:4, 2 * P:3 * P], 8)
                    for n in (4, 5):
                        unit_lo(n, 5 + n)
                    dve.wait_ge(ov_pe, ran * PE_STEPS + 7)
                    dve.tensor_copy(expert_out[:, 0, HALF:D], bank["D"][:, :]).then_inc(ov_dve, 1)

                overflow(dve, l, past, block_dve, held_dve)
                for t in range(NT):
                    n = P if t < 4 else DEC
                    dve.wait_ge(y_in[t % 2], 16 * ((3 - t % 2) * l + (t // 2 + 1)))
                    y = y_rows[0:n, t % 2, :, :]
                    dve.tensor_scalar(y[:, 0, :], y[:, 0, :], w12[0:n, t, 0:1], None, ALU.mult)
                    dve.drain()
                    dve.scalar_tensor_tensor(out=x[0:n, t, :], in0=x[0:n, t, :], scalar=ALPHA, in1=y[:, 0, :], op0=ALU.mult, op1=ALU.add)
                    dve.drain()
                    dve.scalar_tensor_tensor(out=x[0:n, t, :], in0=y[:, 1, :], scalar=w12[0:n, t, 1:2], in1=x[0:n, t, :],
                                             op0=ALU.mult, op1=ALU.add).then_inc(y_used, 1)
                    dve.drain()
                    row_stats(t)
                dve.drain()
                for t in range(NT):
                    ins = dve.bn_aggr(mv[:, t, :], stats[:, t, :, :])
                ins.then_inc(var2, 1)
                dve.wait_ge(sd2, l + 1)
                dve.reciprocal(rs, sd)
                dve.drain()
                dve.wait_ge(table2_in, 32 * l + 32)
                for t in range(NT):
                    ins = layer_norm(t)
                ins.then_inc(x_ready, 1)

        @block.tensor
        def _(pe):
            for b in "ABCDEFGH":
                pe.sem_inc(freed[b], 1)
            pe.wait_ge(boot, 16 * 7)

            def turn(name, l, srcs, i=0):
                wait_free(pe, name, l, i)
                for k, src in enumerate(srcs):
                    ins = pe.transpose(bank_of(name)[:, k * P:(k + 1) * P], src, ident)
                done(ins, name)

            def product(name, col, units, n, last=None):
                out = bank_of(name)[:, 0:n]
                steps = [(slot, k0 + j, j) for slot, k0 in units for j in range(4)]
                for m, (slot, k, j) in enumerate(steps):
                    for a, w in ((xt_hi, w_hi), (xt_hi, w_lo), (xt_lo, w_hi)):
                        ins = pe.matmul(out, a[:, k, col:col + P], w[:, slot, j, 0:n],
                                        start=(m == 0 and a is xt_hi and w is w_hi),
                                        stop=(m == len(steps) - 1 and a is xt_lo))
                    if last is not None and m == 3:
                        ins.then_inc(half_used, 1)
                done(ins, name)

            past = new_past(pe)
            with pe.Fori(0, DEPTH) as l:
                pe.wait_ge(x_ready, l + 1)
                for t in range(NT):
                    for h in range(2):
                        turn(("xt", t, h), l, [x[:, t, (4 * h + k) * P:(4 * h + k + 1) * P] for k in range(4)])
                for g in range(4):
                    for t in range(NT):
                        if g == 0:
                            wait_read(pe, ("xt", t, 1), l)
                        if t == 0:
                            wait_unit(pe, l, 2 * g + 1)
                        wait_free(pe, ("proj", g, t), l)
                        product(("proj", g, t), t * P, [(2 * g % RB, 0), ((2 * g + 1) % RB, 4)], width(2 * g),
                                last=True if t == NT - 1 else None)
                pe.wait_ge(k_done, NT * (l + 1))
                turn("kt0", l, [kv[:, t, 0:P] for t in range(4)])
                pe.wait_ge(att_in, 64 * l + 64)
                turn("kt1", l, [cache[:, 0, :], kv[:, 4, 0:P]])
                pe.wait_ge(tril_done, l + 1)
                turn("wst", l, [ws[:, g, :] for g in range(4)])
                pe.wait_ge(zero_done, 2 * l + 2)
                pe.wait_ge(q_done, NT * (l + 1))

                def weighted_values(t):
                    for j in range(4):
                        pe.wait_ge(exp_done, 9 * NT * l + (9 * t + 2 * j + 2))
                        turn(("pt", t, j), l, [probs[:, t % 2, j, a, b * P:(b + 1) * P] for a in range(2) for b in range(2)])
                        if j:
                            values(t, j - 1)
                    values(t, 3)

                def values(t, j):
                    if j == 0:
                        wait_free(pe, ("o", t), l)
                    wait_read(pe, ("pt", t, j), l)
                    for a in range(2):
                        h = 2 * j + a
                        c = P + h // 4 * 64
                        if t == 0:
                            v = (zeros[:, 0:64], kv[:, 0, c:c + 64])
                        elif t == NT - 1:
                            v = (cache[:, 1, h // 4 * 64:h // 4 * 64 + 64], kv[:, t, c:c + 64])
                        else:
                            v = (kv[:, t - 1, c:c + 64], kv[:, t, c:c + 64])
                        for b in range(2):
                            ins = pe.matmul(bank_of(("o", t))[:, h * 64:(h + 1) * 64], probs_t[:, j % 2, 2 * a + b, :], v[b],
                                            start=(b == 0), stop=(b == 1))
                    if j == 3:
                        done(ins, ("o", t))

                for t in range(NT):
                    turn(("qt", t), l, [q[:, t, j * P:(j + 1) * P] for j in range(4)])
                    if t == 0:
                        wait_read(pe, "kt1", l)
                    wait_read(pe, ("qt", t), l)
                    k0 = t * P if t < NT - 1 else 5 * P
                    for j in range(4):
                        name = ("s", t, j)
                        side, jj = j % 2, j // 2
                        wait_free(pe, name, l)
                        for a in range(2):
                            ins = pe.matmul(bank_of(name)[:, a * 256:(a + 1) * 256],
                                            q_t[64 * side:64 * side + 64, t % 2, 2 * jj + a, :],
                                            keys_t[64 * side:64 * side + 64, k0:k0 + 256], start=True, stop=True)
                        done(ins, name)
                    name = ("gm", t)
                    if t == 0:
                        wait_read(pe, "wst", l)
                        pe.wait_ge(vn_done, NT * (l + 1))
                    wait_free(pe, name, l)
                    for g in range(4):
                        ins = pe.matmul(bank_of(name)[:, g * P:(g + 1) * P], ws_t[:, g, :], gv[:, t, g * P:(g + 1) * P],
                                        start=True, stop=True)
                    done(ins, name)
                    if t:
                        weighted_values(t - 1)
                weighted_values(NT - 1)
                for t in range(NT):
                    for h, v in enumerate((q, u)):
                        pe.wait_ge(norm_done, 2 * NT * l + (2 * t + h + 1))
                        turn(("mt", t, h), l, [v[:, t, k * P:(k + 1) * P] for k in range(4)])
                for c in range(2):
                    for t in range(NT):
                        if c == 0:
                            wait_read(pe, ("mt", t, 1), l)
                        if t == 0:
                            wait_unit(pe, l, 9 + 2 * c)
                        wait_free(pe, ("wo", c, t), l)
                        product(("wo", c, t), t * P, [(2 * c % RB, 0), ((2 * c + 1) % RB, 4)], HALF,
                                last=True if t == NT - 1 else None)
                def logits(t):
                    wait_read(pe, ("rt", t, 1), l)
                    if t == 0:
                        wait_free(pe, "logit", l)
                    for k in range(KT_N):
                        ins = pe.matmul(bank_of("logit")[:, t * NE:(t + 1) * NE], x1_t[:, t % 2, k, :], wrt[:, k, :],
                                        start=(k == 0), stop=(k == KT_N - 1))
                    if t == NT - 1:
                        done(ins, "logit")

                for t in range(NT):
                    pe.wait_ge(x1_ready, NT * l + t + 1)
                    for h in range(2):
                        turn(("rt", t, h), l, [x[:, t, (4 * h + k) * P:(4 * h + k + 1) * P] for k in range(4)])
                    if t:
                        logits(t - 1)
                logits(NT - 1)
                pe.wait_ge(pick_done, l + 1)
                wait_free(pe, "rank", l)
                for t in range(NT + 1):
                    for r in range(min(t + 1, NT)):
                        ins = pe.matmul(bank_of("rank")[:, t * NE:(t + 1) * NE], before if r == t else ones,
                                        pick[:, r * NE:(r + 1) * NE], start=(r == 0), stop=(r == min(t, NT - 1)))
                done(ins, "rank")
                pe.wait_ge(idx_f_done, l + 1)
                wait_free(pe, "index", l)
                pe.sem_inc(held_pe, 1)
                done(pe.transpose(bank_of("index")[:, 0:NE], idx_f[:, :], ident[0:NE, 0:NE]), "index")

                def rows_turn(i, s):
                    pe.wait_ge(rows_in[s], 16 * (l * PAIRS + i + 1))
                    for h in range(2):
                        turn(("xe", s, h), l, [rows[:, s, (4 * h + k) * P:(4 * h + k + 1) * P] for k in range(4)], i)

                def up(i, s):
                    c = SO_MOE + 4 * s
                    for n, name in enumerate((("gate", s), ("up", s))):
                        wait_unit(pe, l, c + 2 * n + 1, i)
                        wait_free(pe, name, l, i)
                        yield product(name, s * P, [((c + 2 * n) % RB, 0), ((c + 2 * n + 1) % RB, 4)], HALF, last=True)

                def hidden_turn(i, s):
                    wait_read(pe, ("up", s), l, i)
                    turn(("ht", s), l, [hidden[:, s, k * P:(k + 1) * P] for k in range(4)], i)

                def down(i, s):
                    wait_read(pe, ("ht", s), l, i)
                    for c in range(2):
                        n = SO_MOE + 8 + 2 * s + c
                        wait_unit(pe, l, n, i)
                        wait_free(pe, (f"down{c}", s), l, i)
                        product((f"down{c}", s), (2 + s) * P, [(n % RB, 0)], HALF)

                rows_turn(0, 0)
                rows_turn(0, 1)

                def pair(i, last=False):
                    wait_read(pe, ("xe", 0, 1), l, i)
                    for _g in up(i, 0):
                        pass
                    wait_read(pe, ("xe", 1, 1), l, i)
                    second = up(i, 1)
                    next(second)
                    hidden_turn(i, 0)
                    next(second)
                    if not last:
                        rows_turn(i + 1, 0)
                    down(i, 0)
                    hidden_turn(i, 1)
                    if not last:
                        rows_turn(i + 1, 1)
                    down(i, 1)

                with pe.Fori(0, PAIRS - 1) as i:
                    pair(i)
                pair(PAIRS - 1, last=True)

                def block_pe(e, b, ran):
                    def turned(out, srcs):
                        for k, src in enumerate(srcs):
                            ins = pe.transpose(out[:, k * P:(k + 1) * P], src, ident)
                        ins.then_inc(ov_pe, 1)

                    def three_pass(out, col, units, after):
                        pe.wait_ge(ov_dve, ran * DVE_STEPS + after)
                        steps = [(slot, k0 + j, j) for slot, k0 in units for j in range(4)]
                        for m, (slot, k, j) in enumerate(steps):
                            for n, (a, w) in enumerate(((xt_hi, w_hi), (xt_hi, w_lo), (xt_lo, w_hi))):
                                ins = pe.matmul(out[:, :], a[:, k, col:col + P], w[:, slot, j, :],
                                                start=m == n == 0, stop=m == len(steps) - 1 and n == 2)
                        ins.then_inc(ov_pe, 1)

                    pe.wait_ge(ov_rows, 16 * (ran + 1))
                    for h in range(2):
                        turned(bank["EF"[h]], [rows[:, 0, (4 * h + k) * P:(4 * h + k + 1) * P] for k in range(4)])
                    three_pass(bank["A"], 0, [(0, 0), (1, 4)], 5)
                    three_pass(bank["B"], 0, [(2, 0), (3, 4)], 7)
                    pe.wait_ge(ov_dve, ran * DVE_STEPS + 8)
                    turned(bank["G"], [hidden[:, 0, k * P:(k + 1) * P] for k in range(4)])
                    for c in range(2):
                        three_pass(bank["CD"[c]], 2 * P, [(c, 0)], 10 + c)

                overflow(pe, l, past, block_pe, held_pe)


_INS = ["x_prompt", "x_sample", "cache_k", "cache_v", "w_in", "sinks", "gm_ln_g", "gm_ln_b", "gm_ws", "gm_bs",
        "out_norm_a", "out_norm_b", "w_o", "ln1_g", "ln1_b", "w_router", "router_bias", "w_gate", "w_up", "w_down",
        "ln2_g", "ln2_b"]
_OUTS = [(1, SEQ, D), (1, DEC, D), (DEPTH, 1, P, 2, 64), (DEPTH, 1, P, 2, 64), (DEPTH, 1, DEC, 2, 64),
         (DEPTH, 1, DEC, 2, 64), (DEPTH, 1, DEC, HALF)]


def constants():
    f = np.float32
    inv = np.power(f(10000.0), -np.arange(32, dtype=f) / f(32)).astype(f)
    pos = np.concatenate([np.arange(SEQ), PAST + np.arange(DEC), np.zeros(ROWS - SEQ - DEC)]).astype(f)
    ang = (pos[:, None] * inv[None, :]).astype(np.float64)
    cos, sin = np.cos(ang), np.sin(ang)
    rope = np.stack([np.concatenate([cos, cos], 1), np.concatenate([-sin, sin], 1)], 1).astype(f)
    mask = np.zeros((3, P, 256), f)
    mask[0, 0:64, 192:] = -BIG
    mask[0, 64:, 0:64] = -BIG
    mask[1] = mask[0]
    mask[1, :, 0:P] = -BIG
    mask[2, :, 192:] = -BIG
    mats = np.zeros((P, 3 * P + 46), f)
    mats[:, 0:P] = np.eye(P)
    mats[:, P:2 * P] = np.triu(np.ones((P, P)), 1)
    mats[:, 2 * P:3 * P] = 1.0
    c = 3 * P
    mats[:, c:c + 16] = np.arange(16, 0, -1)
    mats[:, c + 16:c + 32] = CAP * np.arange(16)
    mats[:, c + 32:c + 36] = np.arange(4, 0, -1)
    mats[:, c + 36:c + 41] = 1.0
    mats[DEC:, c + 40] = 0.0
    mats[DEC:, c + 45] = 1.0
    ints = np.full((P, 2 * NT + NSLOT // P), OOB, np.int32)
    for t in range(NT):
        for j in range(2):
            ints[:, 2 * t + j] = 2 * (t * P + np.arange(P)) + j
    return {"c_rope": rope, "c_mask": mask, "c_mats": mats, "c_ints": ints}


def kernel(**inputs):
    import concourse.bacc as _bacc
    from concourse.bass_utils import run_bass_kernel_spmd as _run

    nc = _bacc.Bacc("TRN2", target_bir_lowering=False, num_devices=1)
    arrays, args = {}, []
    for name in _INS:
        arrays[f"in_{name}"] = np.ascontiguousarray(inputs[name])
    for name, a in constants().items():
        arrays[f"in_{name}"] = a
    for name, a in arrays.items():
        args.append(nc.dram_tensor(name, a.shape, mybir.dt.from_np(a.dtype), kind="ExternalInput").ap())
    for i, shape in enumerate(_OUTS):
        args.append(nc.dram_tensor(f"out_{i}", shape, F32, kind="ExternalOutput").ap())
    build(nc, *args)
    r = _run(nc, [arrays], core_ids=[0])
    return tuple(r.results[0][f"out_{i}"] for i in range(len(_OUTS)))
```

```python
from contextlib import ExitStack

import numpy as np

import concourse.bass as bass
from concourse import mybir

F32 = mybir.dt.float32
F32R = mybir.dt.float32r
I32 = mybir.dt.int32
BF16 = mybir.dt.bfloat16
U32 = mybir.dt.uint32
ALU = mybir.AluOpType
ACT = mybir.ActivationFunctionType
AX = mybir.AxisListType.X

P = 128
D = 1024
KT_N = D // P
SEQ, DEC, PAST = 512, 64, 256
DEPTH = 2
NT = 5
ROWS = NT * P
HALF = 512
NE = 16
NG = 4
EPG = NE // NG
CAP = ROWS
NSLOT = NE * CAP
BLOCKS = CAP // P
ALPHA = float((2 * DEPTH) ** 0.25)
EPS = 1e-5
BIG = 1e30
SCALE = 64 ** -0.5
OOB = 1 << 20

UNITS_PROJ = 8
UNITS_WO = 4
PAIR_UNITS = 12
PAIRS = NE // 2
UNITS = UNITS_PROJ + UNITS_WO + PAIRS * PAIR_UNITS
YB = 4
RB = 4
SO_MOE = UNITS_PROJ + UNITS_WO
OVB = NE * (BLOCKS - 1)


def fill_plan():
    count = dict.fromkeys("ABCDEFGH", 0)
    at = {}

    def fill(name, bank):
        at[name] = (bank, count[bank], 0)
        count[bank] += 1

    for t in range(NT):
        for h in range(2):
            fill(("xt", t, h), "EF"[h])
    for g in range(4):
        for t in range(NT):
            fill(("proj", g, t), "ABCD"[(g * NT + t) % 4])
    fill("kt0", "E")
    fill(("qt", 0), "G")
    fill("kt1", "F")
    fill("wst", "H")
    for t in range(NT + 3):
        if t < NT:
            for j in range(4):
                fill(("s", t, j), "ABCD"[j])
        if t + 1 < NT:
            fill(("qt", t + 1), "H")
        if t == 0:
            for r in range(NT):
                fill(("gm", r), "GH"[r % 2])
        if 4 <= t < NT + 2:
            fill(("logit", t - 4), "H")
            fill(("turned logit", t - 4), "H")
        if t >= 3:
            for c in range(2):
                fill(("wo", c, t - 3), "AB"[c])
        if 1 <= t < NT + 1:
            for j in range(4):
                fill(("pt", t - 1, j), "EF"[j % 2])
            fill(("o", t - 1), "G")
        if 2 <= t < NT + 2:
            for h in range(2):
                fill(("mt", t - 2, h), "EF"[h])
        if 3 <= t < NT + 1:
            for h in range(2):
                fill(("rt", t - 3, h), "CD"[h])
    for t in (NT - 2, NT - 1):
        for h in range(2):
            fill(("rt", t, h), "CD"[h])
        fill(("logit", t), "H")
        fill(("turned logit", t), "H")
    fill("rank", "H")
    fill("index", "H")
    for s in range(2):
        for h in range(2):
            at["xe", s, h] = ("EF"[h], count["EF"[h]] + s, 2)
        for name, bank in (("gate", "A"), ("up", "B"), ("down0", "C"), ("down1", "D"), ("ht", "G")):
            at[name, s] = (bank, count[bank] + s, 2)
    for bank in "EFABCDG":
        count[bank] += 2 * PAIRS
    return at, count


def build(nc, x_prompt, x_sample, cache_k, cache_v, w_in, sinks, gm_ln_g, gm_ln_b, gm_ws, gm_bs,
          out_norm_a, out_norm_b, w_o, ln1_g, ln1_b, w_router, router_bias, w_gate, w_up, w_down,
          ln2_g, ln2_b, c_rope, c_mask, c_ident, c_router, c_ints, c_nowhere,
          y_prompt, y_sample, k_prompt, v_prompt, k_sample, v_sample, gmv_sample):
    FILL, NFILL = fill_plan()
    ctx = ExitStack()
    with ctx:
        def sb(name, shape, dt=F32):
            return ctx.enter_context(nc.sbuf_tensor(name, shape, dt))

        def sem(name):
            return ctx.enter_context(nc.semaphore(name))

        def over(base, name, shape, dt=F32, at=0):
            return nc.alloc_sbuf_tensor_at(name, shape, dt, offset=base + at)

        raw = sb("raw", [P, RB, 4, HALF])
        w_hi = sb("w_hi", [P, RB, 4, HALF], F32R)
        w_lo = sb("w_lo", [P, RB, 4, HALF], F32R)
        x = sb("x", [P, NT, D])
        base_t = nc.sbuf_base
        arena_t = sb("arena_t", [P, 2 * KT_N * ROWS])
        base_m = nc.sbuf_base
        arena_m = sb("arena_m", [P, NT * (3 * HALF + 256)])
        table = sb("table", [P, 4, HALF])
        rope = sb("rope", [P, NT, 2, 64])
        ident = sb("ident", [P, P])[:, :]
        small = sb("small", [P, 400])
        ints = sb("ints", [P, 2 * NT, 2], I32)
        wrt = sb("wrt", [P, KT_N, NE])
        ws = sb("ws", [P, 4, P])
        cache = sb("cache", [P, 2, P])

        xt_hi = over(base_t, "xt_hi", [P, KT_N, ROWS], F32R)
        xt_lo = over(base_t, "xt_lo", [P, KT_N, ROWS], F32R, 4 * KT_N * ROWS)
        keys_hi = over(base_t, "keys_hi", [P, 7 * P], F32R)
        keys_lo = over(base_t, "keys_lo", [P, 7 * P], F32R, at=3584)
        q_hi = over(base_t, "q_hi", [P, 4, P], F32R, at=7168)
        q_lo = over(base_t, "q_lo", [P, 4, P], F32R, at=9216)
        probs = over(base_t, "probs", [P, 2, 4, 2, 256], at=11264)
        probs_t = over(base_t, "probs_t", [P, 2, 4, P], at=27648)
        mask = over(base_t, "mask", [P, 3, 256], at=31744)
        ws_t = over(base_t, "ws_t", [P, 4, P], at=34816)
        consts = over(base_t, "consts", [P, 3 * P + 46 + 8 * NT])
        x1_t = over(base_t, "x1_t", [P, KT_N, P], at=36864)
        logits_t = over(base_t, "logits_t", [NE, P], at=3584)

        QB = 4 * NT * HALF
        q = over(base_m, "q", [P, NT, HALF])
        u = over(base_m, "u", [P, NT, HALF], at=QB)
        gv = over(base_m, "gv", [P, NT, HALF], at=2 * QB)
        kv = over(base_m, "kv", [P, NT, 256], at=3 * QB)
        rope_a = over(base_m, "rope_a", [P, HALF], at=QB + 3 * 4 * HALF)
        rope_b = over(base_m, "rope_b", [P, HALF], at=QB + 4 * 4 * HALF)
        mt_hi = over(base_m, "mt_hi", [P, KT_N, P], F32R, at=2 * QB)
        mt_lo = over(base_m, "mt_lo", [P, KT_N, P], F32R, at=2 * QB + 4 * D)
        squares = over(base_m, "squares", [P, HALF], at=2 * QB + 8 * D)
        ln1_shift = over(base_m, "ln1_shift", [P, 2, NT * HALF])[:, :, 0:HALF]
        rows = over(base_m, "rows", [P, 2, D])
        expert_out = over(base_m, "expert_out", [P, 2, D], at=QB)
        act_gate = over(base_m, "act_gate", [P, 2, HALF], at=2 * QB)
        hidden = over(base_m, "hidden", [P, 2, HALF], at=2 * QB + 8 * HALF)
        y_rows = over(base_m, "y_rows", [P, YB, 2, D])

        before, ones, iota = consts[:, 0:P], consts[:, P:2 * P], consts[:, 2 * P:3 * P]
        c0 = 3 * P
        desc16, slot0 = consts[:, c0:c0 + 16], consts[:, c0 + 16:c0 + 32]
        desc4, valid, invalid = consts[:, c0 + 32:c0 + 36], consts[:, c0 + 36:c0 + 41], consts[:, c0 + 41:c0 + 46]
        parts_f = consts[:, c0 + 46:c0 + 46 + 8 * NT]

        at = [0]

        def sm(*shape):
            n = int(np.prod(shape))
            at[0] += n
            v = small[:, at[0] - n:at[0]]
            if len(shape) == 2:
                return v.rearrange("p (a b) -> p a b", a=shape[0])
            return v

        sink, bs, rbias, eps = sm(8), sm(4), sm(NE), sm(1)
        top, ntop, den, rden = sm(2, 8), sm(2, 8), sm(2, 8), sm(2, 8)
        sink_top, esink = sm(2, 8), sm(2, 8)
        gm_var, gm_sd, gm_rs = sm(4 * NT, 2), sm(4 * NT), sm(4 * NT)
        mv, sd, rs, shift_row = sm(NT, 2), sm(NT), sm(NT), sm(NT)
        sq, rms, rn = sm(NT, 2), sm(NT, 2), sm(NT, 2)
        w12, warm = sm(NT, 2), sm(3)
        shared = sm(4 * NT * 6)
        gm_stats = shared.rearrange("p (a b) -> p a b", b=6)
        stats = shared[:, 0:24].rearrange("p (t h b) -> p t h b", t=2, h=2)
        logits = shared[:, 24:24 + NT * NE]

        def rcols(k, n, name):
            return over(base_m, name, [P, n], at=3 * QB + 320 * k)

        score, sel, in_group, sel2, pick1, pick2, rcol = (
            rcols(k, NT * NE, n) for k, n in enumerate(("score", "sel", "in_group", "sel2", "pick1", "pick2", "rcol")))
        pick = over(base_m, "pick_wide", [P, (NT + 1) * NE], at=3 * QB + 4224)
        work = over(base_m, "work_wide", [P, 6 * NT * NG], at=3 * QB + 4608)
        r20 = [over(base_m, f"r20_{k}", [P, NT * NG], at=3 * QB + 2880 + 96 * k) for k in range(4)]
        r5 = [over(base_m, f"r5_{k}", [P, NT], at=3 * QB + 3840 + 32 * k) for k in range(7)]
        local = over(base_m, "local", [P, 2, 2 * NT], at=3 * QB + 4096)
        first_idx = over(base_m, "first_idx", [P, 2], at=3 * QB + 4192)
        in_slot = over(base_t, "in_slot", [P, 2, 2 * NT, P], BF16, at=11264)

        slots = sb("slots", [P, 2 * NT], I32)
        count_max = sb("count_max", [P, 1], I32)
        idx = sb("idx", [P, NE, 2], I32)
        parts = sb("parts", [P, 2 * NT, 4], BF16)
        cur_src = sb("cur_src", [P, 2], I32)
        cur_res = sb("cur_res", [P, 2], I32)

        ov_pair, ov_src = sb("ov_pair", [P, 2], I32), sb("ov_src", [P, 1], I32)

        x1_dram = nc.dram_tensor("x1_rows", [ROWS, D], F32, kind="Internal").ap()
        y2_dram = nc.dram_tensor("y2_rows", [2 * ROWS, D], F32, kind="Internal").ap()
        slot_dram = nc.dram_tensor("slot_rows", [NSLOT, 2], I32, kind="Internal").ap()

        bank = {b: ctx.enter_context(nc.psum_tensor("bank" + b, [P, HALF], F32)) for b in "ABCDEFGH"}

        filled = {b: sem("filled" + b) for b in "ABCDEFGH"}
        freed = {b: sem("freed" + b) for b in "ABCDEFGH"}
        raw_in = [sem(f"raw_in{i}") for i in range(RB)]
        hi_done = sem("hi_done")
        lo_done = sem("lo_done")
        half_used = sem("half_used")
        x0_in, x1_in, x_in, boot = sem("x0_in"), sem("x1_in"), sem("x_in"), sem("boot")
        go = sem("go")
        held_pool, held_act, held_dve, held_pe, held_sp = (sem("held_" + n) for n in ("pool", "act", "dve", "pe", "sp"))
        x_ready = sem("x_ready")
        layer_in = sem("layer_in")
        ws_in, mask_in, consts_in = sem("ws_in"), sem("mask_in"), sem("consts_in")
        hi_x, hi_m, hi_e, hi_h = sem("hi_x"), sem("hi_m"), sem("hi_e"), sem("hi_h")
        q_done, k_done = sem("q_done"), sem("k_done")
        vn_done = sem("vn_done")
        hi_k, hi_q, tril_done = sem("hi_k"), sem("hi_q"), sem("tril_done")
        top_done, exp_done = sem("top_done"), sem("exp_done")
        norm_done = sem("norm_done")
        kv_out = sem("kv_out")
        ln1_g_in, ln1_b_in, table2_in = sem("ln1_g_in"), sem("ln1_b_in"), sem("table2_in")
        gm_var_done, gm_sd_done, rms_done, var1_done, sd1_done = (
            sem(n) for n in ("gm_var_done", "gm_sd_done", "rms_done", "var1_done", "sd1_done"))
        first_added, var2_done, sd2_done, stats_done, normalised, gained = (
            sem(n) for n in ("first_added", "var2_done", "sd2_done", "stats_done", "normalised", "gained"))
        scaled, weighted = sem("scaled"), sem("weighted")
        x1_ready, x1_out = sem("x1_ready"), sem("x1_out")
        score_done, pick_done, slot_done = sem("score_done"), sem("pick_done"), sem("slot_done")
        slots_init, slots_out, idx_in = sem("slots_init"), sem("slots_out"), sem("idx_in")
        in_slot_done, rows_zero = sem("in_slot_done"), sem("rows_zero")
        cur_done = sem("cur_done")
        rows_in = [sem("rows_in0"), sem("rows_in1")]
        out_sent = [sem("out_sent0"), sem("out_sent1")]
        out_free = sem("out_free")
        y_in = [sem(f"y_in{i}") for i in range(YB)]
        y_used = sem("y_used")
        stores = sem("stores")
        ov_pe, ov_act, ov_dve = sem("ov_pe"), sem("ov_act"), sem("ov_dve")
        ov_unit, ov_idx, ov_rows, ov_sent = sem("ov_unit"), sem("ov_idx"), sem("ov_rows"), sem("ov_sent")

        block = ctx.enter_context(nc.Block())

        HALVES = 6 + 4 * PAIRS
        CUR = 4 * PAIRS

        def nth(name, l, i=0):
            b, base, stride = FILL[name]
            return l * NFILL[b] + (i * stride if stride else 0) + (base + 1)

        def wait_filled(eng, name, l, i=0):
            eng.wait_ge(filled[FILL[name][0]], nth(name, l, i))

        def wait_free(eng, name, l, i=0):
            eng.wait_ge(freed[FILL[name][0]], nth(name, l, i))

        def wait_read(eng, name, l, i=0):
            eng.wait_ge(freed[FILL[name][0]], nth(name, l, i) + 1)

        def bank_of(name):
            return bank[FILL[name][0]]

        def done(ins, name):
            ins.then_inc(filled[FILL[name][0]], 1)

        def read(ins, name):
            ins.then_inc(freed[FILL[name][0]], 1)

        def y_count(l, t):
            return 16 * ((NT + YB - 1 - t % YB) // YB * l + (t // YB + 1))

        def unit_no(l, s, i=0):
            return l * UNITS + s + (i * PAIR_UNITS if s >= SO_MOE else 0)

        def width(s):
            return 256 if s in (2, 3) else HALF

        def wait_slot(act, l, s, i):
            if s < RB:
                return
            old = s - RB
            if old < SO_MOE:
                if old % 2 == 0:
                    act.wait_ge(half_used, l * HALVES + (old // 2 + 1))
                else:
                    wait_filled(act, ("proj", old // 2, NT - 1) if old < UNITS_PROJ else ("wo", (old - UNITS_PROJ) // 2, NT - 1), l)
                return
            old -= SO_MOE
            if old >= PAIR_UNITS:
                raise ValueError("units 0 to 3 of a pair are asked for by split_next")
            if old < 8 and old % 2 == 0:
                act.wait_ge(half_used, l * HALVES + i * 4 + (6 + old // 2 + 1))
            elif old < 8:
                wait_filled(act, (("gate", "up")[old // 2 % 2], old // 4), l, i)

        def split_hi(act, l, s, i=0, after=None):
            act.wait_ge(raw_in[s % RB], l * (UNITS // RB * 16) + (i * (PAIR_UNITS // RB * 16) if s >= SO_MOE else 0)
                        + 16 * (s // RB + 1))
            if after is not None:
                wait_filled(act, after, l, i - 1)
            else:
                wait_slot(act, l, s, i)
            n = width(s)
            act.activation(w_hi[:, s % RB, :, 0:n], raw[:, s % RB, :, 0:n], ACT.Copy).then_inc(hi_done, 1)

        def split_lo(dve, l, s, i=0):
            dve.wait_ge(hi_done, unit_no(l, s, i) + 1)
            n = width(s)
            dve.tensor_tensor(w_lo[:, s % RB, :, 0:n], raw[:, s % RB, :, 0:n],
                              w_hi[:, s % RB, :, 0:n].bitcast(F32), ALU.subtract).then_inc(lo_done, 1)

        def wait_unit(pe, l, s, i=0):
            pe.wait_ge(lo_done, unit_no(l, s, i) + 1 + RB)

        def hi_out(act, name, l, dst, s, i=0):
            wait_filled(act, name, l, i)
            act.activation(dst, bank_of(name)[:, :].rearrange("p (k n) -> p k n", k=4), ACT.Copy).then_inc(s, 1)

        def lo_out(dve, name, l, lo, hi, s, value, i=0):
            dve.wait_ge(s, value)
            read(dve.tensor_tensor(lo, bank_of(name)[:, :].rearrange("p (k n) -> p k n", k=4), hi.bitcast(F32),
                                   ALU.subtract), name)

        def t_cols(buf, h, c):
            return buf[:, 4 * h:4 * h + 4, c * P:(c + 1) * P]

        PE_STEPS, ACT_STEPS, DVE_STEPS = 7, 11, 12

        def overflow(eng, l, past, body, apart, close=None):
            eng.wait_ge(slot_done, l + 1)
            eng.sem_inc(apart, 1)
            most = eng.value_load(count_max[0:1, 0:1], min_val=0, max_val=ROWS)
            with eng.If(most > P):
                ran0 = eng.snap(past, min_val=0, max_val=DEPTH * OVB)
                with eng.Fori(0, NE) as e:
                    with eng.Fori(1, BLOCKS) as b:
                        body(e, b, ran0 + e * (BLOCKS - 1) + b - 1)
                if close is not None:
                    close(ran0 + OVB)
                eng.reg_add(past, past, OVB)

        def new_past(eng):
            past = eng.alloc_register("past")
            eng.reg_mov(past, 0)
            return past

        @block.sync
        def _(sp):
            def load(l, s, src, i=0, n=HALF):
                sp.wait_ge(lo_done, unit_no(l, s, i) + 1)
                if s < UNITS_PROJ:
                    sp.sem_inc(held_sp, 1)
                if s == RB:
                    sp.wait_ge(x_ready, NT * l + 1)
                    sp.sem_inc(held_sp, 1)
                sp.dma_start(raw[:, s % RB, :, 0:n], src.rearrange("(t p) n -> p t n", p=P)) \
                    .then_inc(raw_in[s % RB], 16)

            for dst, src in ((ident[:, :], c_ident), (x[:, 0, :], x_prompt[0, 0:P, :])):
                sp.dma_start(dst, src).then_inc(x0_in, 16)

            past = new_past(sp)
            with sp.Fori(0, DEPTH) as l:
                s = 0
                for c0, n in ((1280, HALF), (HALF, 256), (0, HALF), (768, HALF)):
                    for k in range(2):
                        load(l, s, w_in[l, k * HALF:(k + 1) * HALF, c0:c0 + n], n=n)
                        s += 1
                for c in range(2):
                    for k in range(2):
                        load(l, s, w_o[l, k * HALF:(k + 1) * HALF, c * HALF:(c + 1) * HALF])
                        s += 1
                with sp.Fori(0, PAIRS) as i:
                    s = SO_MOE
                    for e in range(2):
                        for w in (w_gate, w_up):
                            for k in range(2):
                                load(l, s, w[l, 2 * i + e, k * HALF:(k + 1) * HALF, :], i)
                                s += 1
                    for e in range(2):
                        for c in range(2):
                            load(l, s, w_down[l, 2 * i + e, :, c * HALF:(c + 1) * HALF], i)
                            s += 1

                def block_units(e, b, ran):
                    srcs = [w[l, e, k * HALF:(k + 1) * HALF, :] for w in (w_gate, w_up) for k in range(2)]
                    srcs += [w_down[l, e, :, c * HALF:(c + 1) * HALF] for c in range(2)]
                    for n, src in enumerate(srcs):
                        sp.wait_ge(ov_dve, ran * DVE_STEPS + (1, 4, 5, 6, 7, 10)[n])
                        sp.dma_start(raw[:, n % RB, :, :], src.rearrange("(t p) n -> p t n", p=P)).then_inc(ov_unit, 16)

                def units_used(ran):
                    sp.wait_ge(ov_unit, ran * (16 * 6))
                    sp.sem_inc(held_sp, 1)
                    sp.wait_ge(ov_dve, ran * DVE_STEPS)
                    sp.sem_inc(held_sp, 1)

                overflow(sp, l, past, block_units, held_sp, units_used)

            for t in range(NT):
                sp.wait_ge(x_ready, NT * DEPTH + t + 1)
                if t < 4:
                    sp.dma_start(y_prompt[0, t * P:(t + 1) * P, :], x[:, t, :]).then_inc(stores, 16)
                else:
                    sp.dma_start(y_sample[0], x[0:DEC, 4, :]).then_inc(stores, 16)
            sp.wait_ge(stores, 16 * NT)

        @block.gpsimd
        def _(pool):
            def hold(s, v):
                pool.wait_ge(s, v)
                pool.sem_inc(held_pool, 1)

            pool.memset(eps, EPS).then_inc(go, 1)
            hold(go, 1)
            pool.memset(x[DEC:P, 4, :], 0.0).then_inc(go, 1)
            hold(go, 2)
            hold(x0_in, 16 * 2)
            pool.sem_inc(x_ready, 1)
            hold(x1_in, 16)
            pool.sem_inc(x_ready, 1)
            for dst, src in ((rope[:, :, :, :], c_rope.rearrange("(t p) c n -> p t c n", p=P)), (ints[:, :, :], c_ints),
                             (wrt[:, :, :], w_router.rearrange("(k p) e -> p k e", p=P)),
                             (rbias, router_bias.partition_broadcast(P))):
                pool.dma_start(dst, src).then_inc(boot, 16)
            hold(x_in, 16 * 2)
            pool.sem_inc(x_ready, NT - 2)
            pool.sem_inc(out_free, 2)
            past = new_past(pool)
            with pool.Fori(0, DEPTH) as l:
                hold(x_ready, NT * l + NT)
                for dst, src in ((table[:, 0, :], gm_ln_g[l].rearrange("g c -> (g c)").partition_broadcast(P)),
                                 (table[:, 1, :], gm_ln_b[l].rearrange("g c -> (g c)").partition_broadcast(P)),
                                 (table[:, 2, :], out_norm_a[l].partition_broadcast(P)),
                                 (table[:, 3, :], out_norm_b[l].partition_broadcast(P)),
                                 (sink, sinks[l].partition_broadcast(P))):
                    pool.dma_start(dst, src).then_inc(layer_in, 16)
                pool.dma_start(bs, gm_bs[l].rearrange("g p -> p g"), allow_slow_non_contiguous=True).then_inc(layer_in, 16)
                pool.dma_start(slot_dram, c_nowhere).then_inc(slots_init, 16)
                for dst, src in ((ws[:, :, :], gm_ws[l].rearrange("g p q -> p g q")),
                                 (cache[:, 0, :], cache_k[l, 0].rearrange("s h d -> s (h d)")),
                                 (cache[:, 1, :], cache_v[l, 0].rearrange("s h d -> s (h d)"))):
                    pool.dma_start(dst, src).then_inc(ws_in, 16)
                hold(ws_in, 48 * l + 48)
                pool.affine_select(out=ws[:, :, :], in_=ws[:, :, :], compare_op=ALU.is_ge, fill=0.0, base=0,
                                   pattern=[[0, 4], [-1, P]], channel_multiplier=1).then_inc(tril_done, 1)
                hold(k_done, NT * l + NT)
                for dst, src in ((k_prompt[l, 0], kv[:, 3, 0:P]), (v_prompt[l, 0], kv[:, 3, P:256]),
                                 (k_sample[l, 0], kv[0:DEC, 4, 0:P]), (v_sample[l, 0], kv[0:DEC, 4, P:256])):
                    pool.dma_start(dst.rearrange("s h d -> s (h d)"), src).then_inc(kv_out, 16)
                hold(vn_done, NT * l + NT)
                pool.dma_start(gmv_sample[l, 0], gv[0:DEC, 4, :]).then_inc(kv_out, 16)
                pool.dma_start(table[:, 0:2, :], ln1_g[l].rearrange("(a c) -> a c", a=2).partition_broadcast(P)).then_inc(ln1_g_in, 16)
                hold(filled["F"], nth(("mt", 0, 1), l))
                pool.dma_start(ln1_shift, ln1_b[l].rearrange("(a c) -> a c", a=2).partition_broadcast(P)).then_inc(ln1_b_in, 16)
                for t in range(NT):
                    hold(x1_ready, NT * l + t + 1)
                    pool.dma_start(x1_dram[t * P:(t + 1) * P, :], x[:, t, :]).then_inc(x1_out, 16)
                    if t == 1:
                        hold(filled["D"], nth(("s", NT - 1, 3), l))
                        pool.dma_start(consts[:, :], c_router).then_inc(consts_in, 16)
                pool.dma_start(table[:, 0:2, :], ln2_g[l].rearrange("(a c) -> a c", a=2).partition_broadcast(P)).then_inc(table2_in, 16)
                pool.dma_start(table[:, 2:4, :], ln2_b[l].rearrange("(a c) -> a c", a=2).partition_broadcast(P)).then_inc(table2_in, 16)
                hold(rows_zero, l + 1)

                def gather(s):
                    pool.indirect_dma_start(
                        out=rows[:, s, :], out_offset=None, in_=x1_dram,
                        in_offset=bass.IndirectOffsetOnAxis(ap=cur_src[:, s:s + 1].bitcast(U32), axis=0),
                        bounds_check=ROWS - 1, oob_is_err=False).then_inc(rows_in[s], 16)

                def scatter(s):
                    pool.indirect_dma_start(
                        out=y2_dram, out_offset=bass.IndirectOffsetOnAxis(ap=cur_res[:, s:s + 1].bitcast(U32), axis=0),
                        in_=expert_out[:, s, :], in_offset=None,
                        bounds_check=2 * ROWS - 1, oob_is_err=False).then_inc(out_sent[s], 16)

                hold(x1_out, 16 * NT * (l + 1))
                hold(cur_done, l * CUR + 2)
                for s in range(2):
                    gather(s)
                hold(slots_init, 16 * l + 16)
                hold(slot_done, l + 1)
                for c in range(2 * NT):
                    pool.indirect_dma_start(
                        out=slot_dram, out_offset=bass.IndirectOffsetOnAxis(ap=slots[:, c:c + 1].bitcast(U32), axis=0),
                        in_=ints[:, c, :], in_offset=None, bounds_check=NSLOT - 1, oob_is_err=False) \
                        .then_inc(slots_out, 16)
                hold(slots_out, 16 * 2 * NT * (l + 1))
                pool.dma_start(idx[:, :, :], slot_dram.rearrange("(e s) o -> s e o", e=NE)[0:P, :, :],
                               allow_slow_non_contiguous=True).then_inc(idx_in, 16)
                hold(idx_in, 16 * l + 16)

                def pair(i, last=False):
                    n0 = l * CUR + i * 4 + 2
                    if not last:
                        for s in range(2):
                            hold(filled["F"], nth(("xe", s, 1), l, i))
                            hold(rows_in[s], 16 * (l * PAIRS + i + 1))
                            pool.tensor_copy(cur_src[:, s:s + 1], idx[:, bass.ds(2 * i + 2 + s, 1), 1]).then_inc(cur_done, 1)
                        hold(cur_done, n0 + 2)
                        for s in range(2):
                            gather(s)
                    for s in range(2):
                        pool.tensor_copy(cur_res[:, s:s + 1], idx[:, bass.ds(2 * i + s, 1), 0]).then_inc(cur_done, 1)
                    hold(cur_done, n0 + (2 if last else 4))
                    for s in range(2):
                        for c in range(2):
                            hold(freed["CD"[c]], nth((f"down{c}", s), l, i) + 1)
                        scatter(s)
                    for s in range(2):
                        hold(out_sent[s], 16 * (l * PAIRS + i + 1))
                        pool.sem_inc(out_free, 1)

                with pool.Fori(0, PAIRS - 1) as i:
                    pair(i)
                pair(PAIRS - 1, last=True)

                def block_rows(e, b, ran):
                    pool.dma_start(ov_pair[:, :], slot_dram[bass.ds(e * CAP + b * P, P), :]).then_inc(ov_idx, 16)
                    hold(ov_dve, ran * DVE_STEPS + 1)
                    pool.indirect_dma_start(
                        out=rows[:, 0, :], out_offset=None, in_=x1_dram,
                        in_offset=bass.IndirectOffsetOnAxis(ap=ov_src[:, 0:1].bitcast(U32), axis=0),
                        bounds_check=ROWS - 1, oob_is_err=False).then_inc(ov_rows, 16)
                    hold(ov_act, ran * ACT_STEPS + 11)
                    hold(ov_dve, ran * DVE_STEPS + 12)
                    pool.indirect_dma_start(
                        out=y2_dram, out_offset=bass.IndirectOffsetOnAxis(ap=ov_pair[:, 0:1].bitcast(U32), axis=0),
                        in_=expert_out[:, 0, :], in_offset=None,
                        bounds_check=2 * ROWS - 1, oob_is_err=False).then_inc(ov_sent, 16)
                    hold(ov_sent, 16 * (ran + 1))

                overflow(pool, l, past, block_rows, held_pool)

                def add_first(t):
                    n = P if t < 4 else DEC
                    hold(weighted, (NT - 1) * l + t)
                    pool.drain()
                    pool.tensor_tensor(x[0:n, t, :], x[0:n, t, :], y_rows[0:n, t % YB, 0, :], ALU.add).then_inc(first_added, 1)

                def shift(t):
                    hold(gained, (NT - 1) * l + t)
                    pool.drain()
                    xt = x[:, t, :].rearrange("p (a c) -> p a c", a=2)
                    pool.tensor_tensor(xt, xt, table[:, 2:4, :], ALU.add).then_inc(x_ready, 1)

                add_first(1)
                add_first(2)
                hold(table2_in, 32 * l + 32)
                for t in range(1, NT):
                    if t + 2 < NT:
                        add_first(t + 2)
                    shift(t)

            pool.wait_ge(kv_out, 16 * 5 * DEPTH)

        @block.scalar
        def _(act):
            act.wait_ge(go, 1)
            past = new_past(act)

            def rows_hi_x(l, t):
                for h in range(2):
                    hi_out(act, ("xt", t, h), l, t_cols(xt_hi, h, t), hi_x)

            for t in range(NT):
                rows_hi_x(0, t)
                if t == 0:
                    split_hi(act, 0, 0)
                    act.wait_ge(raw_in[1], 16)
                    act.sem_inc(held_act, 1)
                    act.dma_start(x[:, 1, :], x_prompt[0, P:2 * P, :]).then_inc(x1_in, 16)
                    act.dma_start(x[:, 2:4, :], x_prompt[0, 2 * P:SEQ, :].rearrange("(t p) d -> p t d", p=P)).then_inc(x_in, 16)
                    act.dma_start(x[0:DEC, 4, :], x_sample[0]).then_inc(x_in, 16)
                    split_hi(act, 0, 1)
            split_hi(act, 0, 2)
            split_hi(act, 0, 3)

            with act.Fori(0, DEPTH) as l:

                def gelu(g, dst, t):
                    wait_filled(act, ("proj", g, t), l)
                    read(act.activation(dst[:, t, :], bank_of(("proj", g, t))[:, :], ACT.Gelu), ("proj", g, t))

                for t in range(4):
                    gelu(0, gv, t)
                split_hi(act, l, 4)
                gelu(0, gv, 4)
                split_hi(act, l, 5)
                act.wait_ge(gm_var_done, l + 1)
                act.activation(gm_sd, gm_var[:, :, 1], ACT.Sqrt, bias=eps).then_inc(gm_sd_done, 1)
                for s in (6, 7, 8, 9):
                    split_hi(act, l, s)
                act.wait_ge(q_done, NT * l + NT)
                for t in range(4):
                    gelu(3, u, t)
                split_hi(act, l, 10)
                wait_filled(act, ("proj", 3, NT - 1), l)
                act.sem_inc(held_act, 1)
                act.dma_start(mask[:, :, :], c_mask.rearrange("c p n -> p c n")).then_inc(mask_in, 16)
                gelu(3, u, 4)
                wait_filled(act, "kt0", l)
                act.activation(keys_hi[:, P:5 * P], bank_of("kt0")[:, :], ACT.Copy).then_inc(hi_k, 1)

                def queries_out(t):
                    wait_filled(act, ("qt", t), l)
                    act.activation(q_hi[:, :, :], bank_of(("qt", t))[:, :].rearrange("p (a n) -> p a n", a=4), ACT.Copy).then_inc(hi_q, 1)

                def probs_out(t, js):
                    for j in js:
                        wait_filled(act, ("pt", t, j), l)
                        read(act.activation(probs_t[:, j % 2, :, :], bank_of(("pt", t, j))[:, :].rearrange("p (a n) -> p a n", a=4),
                                            ACT.Copy), ("pt", t, j))

                def exponentials(t):
                    act.wait_ge(top_done, NT * l + t + 1)
                    for h in range(8):
                        act.activation(probs[:, t % 2, h // 2, h % 2, :], probs[:, t % 2, h // 2, h % 2, :], ACT.Exp,
                                       bias=ntop[:, t % 2, h:h + 1], accum_out=den[:, t % 2, h:h + 1]).then_inc(exp_done, 1)
                    act.activation(esink[:, t % 2, :], sink_top[:, t % 2, :], ACT.Exp).then_inc(exp_done, 1)

                def sums_of_squares(t):
                    if t == 0:
                        wait_read(act, ("gm", NT - 1), l)
                        act.sem_inc(held_act, 1)
                        act.wait_ge(kv_out, 80 * l + 80)
                        act.sem_inc(held_act, 1)
                    wait_read(act, ("o", t), l)
                    act.activation(squares[:, :], q[:, t, :], ACT.Square, scale=HALF ** -0.5,
                                   accum_out=sq[:, t, 0:1])
                    act.drain()
                    act.activation(squares[:, :], u[:, t, :], ACT.Square, scale=HALF ** -0.5, accum_out=sq[:, t, 1:2])
                    act.drain()
                    act.activation(rms[:, t, :], sq[:, t, :], ACT.Sqrt, bias=eps).then_inc(rms_done, 1)

                def mixed_hi(t):
                    if t:
                        wait_filled(act, ("wo", 1, t - 1), l)
                        act.sem_inc(held_act, 1)
                    for h in range(2):
                        hi_out(act, ("mt", t, h), l, mt_hi[:, 4 * h:4 * h + 4, :], hi_m)

                def router_rows_out(t):
                    for h in range(2):
                        wait_filled(act, ("rt", t, h), l)
                        read(act.activation(x1_t[:, 4 * h:4 * h + 4, :],
                                            bank_of(("rt", t, h))[:, :].rearrange("p (a n) -> p a n", a=4), ACT.Copy), ("rt", t, h))

                queries_out(0)
                for part in (keys_hi, keys_lo):
                    act.activation(part[:, 0:P], ident, ACT.Copy, scale=0.0)
                wait_filled(act, "kt1", l)
                act.activation(keys_hi[:, 5 * P:7 * P], bank_of("kt1")[:, 0:2 * P], ACT.Copy).then_inc(hi_k, 1)
                wait_filled(act, "wst", l)
                read(act.activation(ws_t[:, :, :], bank_of("wst")[:, :].rearrange("p (g n) -> p g n", g=4), ACT.Copy), "wst")
                split_hi(act, l, 11)
                for t in range(NT + 3):
                    if t + 1 < NT:
                        queries_out(t + 1)
                    if t == 0:
                        act.activation(warm[:, 2:3], eps, ACT.Exp)
                    if 1 <= t < 3:
                        probs_out(t - 1, range(4))
                    if t < NT:
                        exponentials(t)
                    if 3 <= t < NT + 1:
                        probs_out(t - 1, range(2))
                    if t == NT + 1:
                        mixed_hi(t - 2)
                    if t == NT + 2:
                        router_rows_out(NT - 2)
                    if t >= 3:
                        act.wait_ge(var1_done, NT * l + t - 2)
                        act.activation(sd[:, t - 3:t - 2], mv[:, t - 3, 1:2], ACT.Sqrt, bias=eps).then_inc(sd1_done, 1)
                    if 3 <= t < NT + 1:
                        probs_out(t - 1, range(2, 4))
                    if 2 <= t < NT + 1:
                        mixed_hi(t - 2)
                    if t == NT + 2:
                        split_hi(act, l, 12)
                        act.activation(warm[:, 1:2], eps, ACT.Sigmoid)
                    if t >= 3 and t != NT + 1:
                        router_rows_out(t - 3)
                    if 1 <= t < NT + 1:
                        sums_of_squares(t - 1)
                act.wait_ge(kv_out, 80 * l + 80)
                act.sem_inc(held_act, 1)
                wait_read(act, ("turned logit", NT - 1), l)
                act.activation(score[:, :], logits, ACT.Sigmoid).then_inc(score_done, 1)
                for s in (13, 14, 15):
                    split_hi(act, l, s)
                act.wait_ge(x1_out, 16 * NT * (l + 1))
                act.sem_inc(held_act, 1)
                for t in range(NT):
                    ins = act.activation(x[:, t, :], x[:, t, :], ACT.Copy, scale=ALPHA)
                ins.then_inc(scaled, 1)

                def rows_hi(i, s):
                    for h in range(2):
                        hi_out(act, ("xe", s, h), l, t_cols(xt_hi, h, s), hi_e, i)

                def gate(i, s):
                    wait_filled(act, ("gate", s), l, i)
                    read(act.activation(act_gate[:, s, :], bank_of(("gate", s))[:, :], ACT.Silu), ("gate", s))

                def hidden_hi(i, s):
                    hi_out(act, ("ht", s), l, xt_hi[:, 0:4, (2 + s) * P:(3 + s) * P], hi_h, i)

                def out0(i, s):
                    wait_filled(act, ("down0", s), l, i)
                    act.wait_ge(out_free, l * NE + 2 * i + (s + 1))
                    read(act.activation(expert_out[:, s, 0:HALF], bank_of(("down0", s))[:, :], ACT.Copy), ("down0", s))

                rows_hi(0, 0)
                rows_hi(0, 1)

                def pair(i, last=False):
                    c = SO_MOE
                    split_hi(act, l, c + 4, i)
                    split_hi(act, l, c + 5, i)
                    gate(i, 0)
                    split_hi(act, l, c + 6, i)
                    split_hi(act, l, c + 7, i)
                    split_hi(act, l, c + 8, i)
                    split_hi(act, l, c + 9, i)
                    hidden_hi(i, 0)
                    gate(i, 1)
                    split_hi(act, l, c + 10, i)
                    split_hi(act, l, c + 11, i)
                    if not last:
                        rows_hi(i + 1, 0)
                        split_hi(act, l, c, i + 1, after=("down0", 0))
                    out0(i, 0)
                    hidden_hi(i, 1)
                    if not last:
                        rows_hi(i + 1, 1)
                        split_hi(act, l, c + 1, i + 1, after=("down1", 0))
                        split_hi(act, l, c + 2, i + 1, after=("down0", 1))
                    out0(i, 1)
                    if not last:
                        split_hi(act, l, c + 3, i + 1, after=("down1", 1))

                with act.Fori(0, PAIRS - 1) as i:
                    pair(i)
                pair(PAIRS - 1, last=True)

                def block_act(e, b, ran):
                    def hi(dst, src, after):
                        act.wait_ge(ov_pe, ran * PE_STEPS + after)
                        act.activation(dst, src, ACT.Copy).then_inc(ov_act, 1)

                    def unit_hi(n):
                        act.wait_ge(ov_unit, 16 * (ran * 6 + n + 1))
                        act.activation(w_hi[:, n % RB, :, :], raw[:, n % RB, :, :], ACT.Copy).then_inc(ov_act, 1)

                    for h in range(2):
                        hi(t_cols(xt_hi, h, 0), bank["EF"[h]][:, :].rearrange("p (k n) -> p k n", k=4), 1 + h)
                    for n in range(4):
                        unit_hi(n)
                    act.wait_ge(ov_pe, ran * PE_STEPS + 3)
                    act.activation(act_gate[:, 0, :], bank["A"][:, :], ACT.Silu).then_inc(ov_act, 1)
                    hi(xt_hi[:, 0:4, 2 * P:3 * P], bank["G"][:, :].rearrange("p (k n) -> p k n", k=4), 5)
                    for n in (4, 5):
                        unit_hi(n)
                    act.wait_ge(ov_pe, ran * PE_STEPS + 6)
                    act.activation(expert_out[:, 0, 0:HALF], bank["C"][:, :], ACT.Copy).then_inc(ov_act, 1)
                    act.wait_ge(ov_sent, 16 * (ran + 1))

                overflow(act, l, past, block_act, held_act)
                with act.If(l < DEPTH - 1):
                    for s in range(RB):
                        wait_filled(act, (f"down{s % 2}", s // 2), l, PAIRS - 1)
                        split_hi(act, l + 1, s)
                act.activation(warm[:, 0:1], eps, ACT.Sqrt)
                act.wait_ge(out_free, NE * (l + 1) + 2)
                for t in range(YB):
                    n = P if t < 4 else DEC
                    act.dma_start(y_rows[0:n, t % YB, :, :],
                                  y2_dram[2 * P * t:2 * P * t + 2 * n, :].rearrange("(p j) n -> p j n", j=2)).then_inc(y_in[t % YB], 16)

                def weigh(t):
                    n = P if t < 4 else DEC
                    act.wait_ge(y_in[t % YB], y_count(l, t))
                    act.activation(y_rows[0:n, t % YB, 0, :], y_rows[0:n, t % YB, 0, :], ACT.Copy,
                                   scale=w12[0:n, t, 0:1]).then_inc(weighted, 1)

                def tail(more):
                    weigh(1)
                    for t in range(NT):
                        if more and t == 1:
                            rows_hi_x(l + 1, 0)
                        act.wait_ge(var2_done, NT * l + t + 1)
                        act.activation(sd[:, t:t + 1], mv[:, t, 1:2], ACT.Sqrt, bias=eps).then_inc(sd2_done, 1)
                        act.wait_ge(stats_done, NT * l + t + 1)
                        act.activation(x[:, t, :], x[:, t, :], ACT.Identity, bias=shift_row[:, t:t + 1],
                                       scale=rs[:, t:t + 1]).then_inc(normalised, 1)
                        if t == 0:
                            act.wait_ge(y_used, NT * l + 1)
                            act.dma_start(y_rows[0:DEC, 0, :, :],
                                          y2_dram[8 * P:8 * P + 2 * DEC, :].rearrange("(p j) n -> p j n", j=2)).then_inc(y_in[0], 16)
                        if t == 0:
                            weigh(2)
                        if t < 2:
                            weigh(t + 3)
                        if more and t > 1:
                            rows_hi_x(l + 1, t - 1)
                    if more:
                        rows_hi_x(l + 1, NT - 1)

                with act.If(l < DEPTH - 1):
                    tail(True)
                with act.If(l > DEPTH - 2):
                    tail(False)

        @block.vector
        def _(dve):
            dve.sem_inc(lo_done, RB)
            past = new_past(dve)

            def heads(ap, n):
                return ap.rearrange("p (h c d) -> p h c d", h=n, c=2)

            def rotate(psum, n, t, dst, name):
                w = n * 64
                cos = rope[:, t, 0, :].unsqueeze(1).to_broadcast([P, n, 64])
                sin = rope[:, t, 1, :].rearrange("p (c d) -> p c d", c=2)
                a, b = rope_a[:, 0:w], rope_b[:, 0:w]
                dve.tensor_tensor(a.rearrange("p (h d) -> p h d", h=n), psum.rearrange("p (h d) -> p h d", h=n), cos, ALU.mult)
                src, dst4 = heads(psum, n), heads(b, n)
                dve.tensor_tensor(dst4[:, :, 0, :], src[:, :, 1, :], sin[:, 0, :].unsqueeze(1).to_broadcast([P, n, 32]), ALU.mult)
                last = dve.tensor_tensor(dst4[:, :, 1, :], src[:, :, 0, :], sin[:, 1, :].unsqueeze(1).to_broadcast([P, n, 32]), ALU.mult)
                if name is not None:
                    read(last, name)
                dve.drain()
                if n == 8:
                    a, b = (v.rearrange("p (a j d) -> p a j d", a=2, j=4) for v in (a, b))
                    dst = dst.rearrange("p (j a d) -> p a j d", a=2, j=4)
                return dve.tensor_tensor(dst, a, b, ALU.add)

            def row_stats(t):
                for h in range(2):
                    dve.bn_stats(stats[:, t % 2, h, :], x[:, t, h * HALF:(h + 1) * HALF])
                dve.drain()
                return dve.bn_aggr(mv[:, t, :], stats[:, t % 2, :, :])

            def lo_rows(l, name, h, c, s, value, i=0):
                lo_out(dve, name, l, t_cols(xt_lo, h, c), t_cols(xt_hi, h, c), s, value, i)

            def rows_lo_x(l, t):
                for h in range(2):
                    lo_rows(l, ("xt", t, h), h, t, hi_x, 2 * NT * l + (2 * t + h + 1))

            for t in range(NT):
                rows_lo_x(0, t)
                if t == 0:
                    split_lo(dve, 0, 0)
                    split_lo(dve, 0, 1)
            split_lo(dve, 0, 2)
            split_lo(dve, 0, 3)
            dve.wait_ge(boot, 16 * 4)
            dve.sem_inc(held_dve, 1)

            with dve.Fori(0, DEPTH) as l:
                for t in range(NT):
                    wait_read(dve, ("proj", 0, t), l)
                    for g in range(4):
                        dve.bn_stats(gm_stats[:, 4 * t + g, :], gv[:, t, g * P:(g + 1) * P])
                    if t == 3:
                        split_lo(dve, l, 4)
                split_lo(dve, l, 5)
                dve.drain()
                for c in range(4 * NT):
                    ins = dve.bn_aggr(gm_var[:, c, :], gm_stats[:, c, :])
                ins.then_inc(gm_var_done, 1)
                for t in range(NT):
                    name = ("proj", 1, t)
                    wait_filled(dve, name, l)
                    dve.tensor_copy(kv[:, t, P:256], bank_of(name)[:, P:256])
                    rotate(bank_of(name)[:, 0:P], 2, t, kv[:, t, 0:P], name).then_inc(k_done, 1)
                    dve.drain()
                split_lo(dve, l, 6)
                split_lo(dve, l, 7)
                dve.wait_ge(layer_in, 96 * l + 96)
                dve.sem_inc(held_dve, 1)
                for t in range(NT):
                    name = ("proj", 2, t)
                    wait_filled(dve, name, l)
                    rotate(bank_of(name)[:, :], 8, t, q[:, t, :], name).then_inc(q_done, 1)
                    if t == 0:
                        dve.wait_ge(gm_sd_done, l + 1)
                        dve.reciprocal(gm_rs, gm_sd)
                        dve.drain()
                    for g in range(4):
                        c = 4 * t + g
                        part = gv[:, t, g * P:(g + 1) * P]
                        dve.tensor_scalar(part, part, gm_var[:, c, 0:1], gm_rs[:, c:c + 1], ALU.subtract, ALU.mult)
                    dve.drain()
                    dve.tensor_tensor(gv[:, t, :], gv[:, t, :], table[:, 0, :], ALU.mult)
                    dve.drain()
                    dve.tensor_tensor(gv[:, t, :], gv[:, t, :], table[:, 1, :], ALU.add).then_inc(vn_done, 1)
                split_lo(dve, l, 8)
                split_lo(dve, l, 9)

                def attention_out(t):
                    dve.wait_ge(exp_done, 9 * NT * l + 9 * (t + 1))
                    dve.tensor_tensor(den[:, t % 2, :], den[:, t % 2, :], esink[:, t % 2, :], ALU.add)
                    dve.drain()
                    dve.reciprocal(rden[:, t % 2, :], den[:, t % 2, :])
                    dve.drain()
                    wait_filled(dve, ("o", t), l)
                    read(dve.tensor_tensor(q[:, t, :].rearrange("p (h d) -> p h d", h=8),
                                           bank_of(("o", t))[:, :].rearrange("p (h d) -> p h d", h=8),
                                           rden[:, t % 2, :].unsqueeze(2).to_broadcast([P, 8, 64]), ALU.mult), ("o", t))

                def scores_out(t):
                    m = 1 if t == 0 else 2 if t == NT - 1 else 0
                    if t >= 2:
                        wait_filled(dve, ("pt", t - 2, 3), l)
                    for j in range(4):
                        name = ("s", t, j)
                        wait_filled(dve, name, l)
                        read(dve.scalar_tensor_tensor(
                            out=probs[:, t % 2, (0, 2, 1, 3)[j], :, :], in0=bank_of(name)[:, :].rearrange("p (a n) -> p a n", a=2),
                            scalar=SCALE, in1=mask[:, m, :].unsqueeze(1).to_broadcast([P, 2, 256]),
                            op0=ALU.mult, op1=ALU.add), name)
                    dve.drain()
                    dve.tensor_reduce(top[:, t % 2, :], probs[:, t % 2, :, :, :].rearrange("p j a n -> p (j a) n"), AX, ALU.max)
                    dve.drain()
                    dve.tensor_tensor(top[:, t % 2, :], top[:, t % 2, :], sink, ALU.max)
                    dve.drain()
                    dve.tensor_scalar(ntop[:, t % 2, :], top[:, t % 2, :], -1.0, None, ALU.mult)
                    dve.tensor_tensor(sink_top[:, t % 2, :], sink, top[:, t % 2, :], ALU.subtract).then_inc(top_done, 1)

                def gmlp_out(n):
                    name = ("gm", n)
                    wait_filled(dve, name, l)
                    if n == 0:
                        wait_read(dve, ("proj", 3, NT - 1), l)
                    for g in (n,) if n < 4 else range(4):
                        if n < 4:
                            part = u[:, 0:4, g * P:(g + 1) * P]
                            product = bank_of(name)[:, :].rearrange("p (t c) -> p t c", t=4)
                        else:
                            part, product = u[:, 4, g * P:(g + 1) * P], bank_of(name)[:, g * P:(g + 1) * P]
                        ins = dve.scalar_tensor_tensor(out=part, in0=product, scalar=bs[:, g:g + 1], in1=part,
                                                       op0=ALU.add, op1=ALU.mult)
                    read(ins, name)

                def rms_norm(t):
                    dve.wait_ge(rms_done, NT * l + t + 1)
                    dve.reciprocal(rn[:, t, :], rms[:, t, :])
                    dve.drain()
                    for b, v in enumerate((q, u)):
                        dve.scalar_tensor_tensor(out=v[:, t, :], in0=v[:, t, :], scalar=rn[:, t, b:b + 1],
                                                 in1=table[:, 2 + b, :], op0=ALU.mult, op1=ALU.mult).then_inc(norm_done, 1)

                def mixed_out(t):
                    for c in range(2):
                        name = ("wo", c, t)
                        wait_filled(dve, name, l)
                        part = x[:, t, c * HALF:(c + 1) * HALF]
                        read(dve.scalar_tensor_tensor(out=part, in0=part, scalar=ALPHA, in1=bank_of(name)[:, :],
                                                      op0=ALU.mult, op1=ALU.add), name)
                    dve.drain()

                def layer_norm(t):
                    row_stats(t).then_inc(var1_done, 1)
                    dve.wait_ge(sd1_done, NT * l + t + 1)
                    dve.reciprocal(rs[:, t:t + 1], sd[:, t:t + 1])
                    dve.drain()
                    dve.tensor_scalar(x[:, t, :], x[:, t, :], mv[:, t, 0:1], rs[:, t:t + 1], ALU.subtract, ALU.mult)
                    dve.drain()
                    xt = x[:, t, :].rearrange("p (a c) -> p a c", a=2)
                    if t == 0:
                        dve.wait_ge(ln1_g_in, 16 * l + 16)
                    dve.tensor_tensor(xt, xt, table[:, 0:2, :], ALU.mult)
                    dve.drain()
                    if t == 0:
                        dve.wait_ge(ln1_b_in, 16 * l + 16)
                    dve.tensor_tensor(xt, xt, ln1_shift, ALU.add).then_inc(x1_ready, 1)

                def mixed_lo(t):
                    for h in range(2):
                        lo_out(dve, ("mt", t, h), l, mt_lo[:, 4 * h:4 * h + 4, :], mt_hi[:, 4 * h:4 * h + 4, :], hi_m,
                               2 * NT * l + (2 * t + h + 1))

                def expert_logits_out(t):
                    wait_filled(dve, ("logit", t), l)
                    read(dve.tensor_copy(logits_t[:, :], bank_of(("logit", t))[0:NE, 0:P]), ("logit", t))

                def logits_out(t):
                    name = ("turned logit", t)
                    wait_filled(dve, name, l)
                    read(dve.tensor_copy(logits[:, t * NE:(t + 1) * NE], bank_of(name)[:, 0:NE]), name)

                def keys_lo_out(name, n, a, b):
                    dve.wait_ge(hi_k, 2 * l + n)
                    read(dve.tensor_tensor(keys_lo[:, a:b], bank_of(name)[:, 0:b - a], keys_hi[:, a:b].bitcast(F32),
                                           ALU.subtract), name)

                def queries_lo_out(t):
                    lo_out(dve, ("qt", t), l, q_lo[:, :, :], q_hi[:, :, :], hi_q, NT * l + t + 1)

                keys_lo_out("kt0", 1, P, 5 * P)
                queries_lo_out(0)
                keys_lo_out("kt1", 2, 5 * P, 7 * P)
                dve.wait_ge(mask_in, 16 * l + 16)
                dve.sem_inc(held_dve, 1)
                for t in range(NT + 3):
                    if t < NT:
                        scores_out(t)
                    if t + 1 < NT:
                        queries_lo_out(t + 1)
                    if t == 0:
                        for r in range(NT):
                            gmlp_out(r)
                    if 4 <= t < NT + 2:
                        expert_logits_out(t - 4)
                    if 2 <= t < NT + 2:
                        rms_norm(t - 2)
                    if t >= 3:
                        mixed_out(t - 3)
                    if t == NT + 1:
                        mixed_lo(t - 2)
                    if t >= 3:
                        layer_norm(t - 3)
                    if 4 <= t < NT + 2:
                        logits_out(t - 4)
                    if 1 <= t < NT + 1:
                        attention_out(t - 1)
                    if t == 1:
                        split_lo(dve, l, 10)
                        split_lo(dve, l, 11)
                    if 2 <= t < NT + 1:
                        mixed_lo(t - 2)
                expert_logits_out(NT - 2)
                logits_out(NT - 2)
                dve.drain()
                dve.memset(rows[:, :, :], 0.0).then_inc(rows_zero, 1)
                split_lo(dve, l, 12)
                expert_logits_out(NT - 1)
                logits_out(NT - 1)

                dve.wait_ge(consts_in, 16 * l + 16)
                dve.tensor_copy(parts.rearrange("p a b -> p (a b)"), parts_f)
                dve.wait_ge(score_done, l + 1)
                sel3 = sel[:, :].rearrange("p (t e) -> p t e", t=NT)
                score3 = score[:, :].rearrange("p (t e) -> p t e", t=NT)
                dve.memset(pick[:, NT * NE:], 0.0)
                dve.tensor_tensor(sel3, score3, rbias.unsqueeze(1).to_broadcast([P, NT, NE]), ALU.add)
                dve.drain()
                s4 = sel[:, :].rearrange("p (a b) -> p a b", b=EPG)
                best, low, group, g_eq = (r[:, :] for r in r20)
                sums = work[:, 0:6 * NT * NG].rearrange("p (a b) -> p a b", b=6)
                dve.tensor_tensor(sums[:, :, 0:2], s4[:, :, 0:2], s4[:, :, 2:4], ALU.add)
                dve.tensor_tensor(sums[:, :, 2:4], s4[:, :, 0::2], s4[:, :, 1::2], ALU.add)
                dve.tensor_tensor(sums[:, :, 4], s4[:, :, 0], s4[:, :, 3], ALU.add)
                dve.tensor_tensor(sums[:, :, 5], s4[:, :, 1], s4[:, :, 2], ALU.add)
                dve.drain()
                dve.tensor_reduce(group, sums, AX, ALU.max)
                dve.drain()

                def first_max(dst, src, n, order, tmp, m):
                    s3, d3, t3 = (v.rearrange("p (a b) -> p a b", b=n) for v in (src, dst, tmp))
                    dve.tensor_reduce(m, s3, AX, ALU.max)
                    dve.drain()
                    dve.tensor_tensor(t3, s3, m.unsqueeze(2).to_broadcast([P, NT, n]), ALU.is_equal)
                    dve.drain()
                    dve.tensor_tensor(t3, t3, order.unsqueeze(1).to_broadcast([P, NT, n]), ALU.mult)
                    dve.drain()
                    dve.tensor_reduce(m, t3, AX, ALU.max)
                    dve.drain()
                    dve.tensor_tensor(d3, t3, m.unsqueeze(2).to_broadcast([P, NT, n]), ALU.is_equal)
                    dve.drain()

                ma, s1, s2, ssum, srec, sl1, sl2 = (r[:, :] for r in r5[0:7])
                first_max(best, group, NG, desc4, g_eq, ma)
                dve.tensor_scalar(low, best, BIG, -BIG, ALU.mult, ALU.add)
                ing = in_group[:, :].rearrange("p (a b) -> p a b", b=EPG)
                dve.tensor_tensor(ing, s4, best.unsqueeze(2).to_broadcast([P, NT * NG, EPG]), ALU.mult)
                dve.drain()
                dve.tensor_tensor(ing, ing, low.unsqueeze(2).to_broadcast([P, NT * NG, EPG]), ALU.add)
                dve.drain()
                first_max(pick1[:, :], in_group[:, :], NE, desc16, work[:, 0:NT * NE], ma)
                dve.scalar_tensor_tensor(out=sel2[:, :], in0=pick1[:, :], scalar=-3 * BIG, in1=in_group[:, :], op0=ALU.mult, op1=ALU.add)
                dve.drain()
                first_max(pick2[:, :], sel2[:, :], NE, desc16, work[:, 0:NT * NE], ma)
                ok = valid.unsqueeze(2).to_broadcast([P, NT, NE])
                for v in (pick1, pick2):
                    v3 = v[:, :].rearrange("p (t e) -> p t e", t=NT)
                    dve.tensor_tensor(v3, v3, ok, ALU.mult)
                dve.drain()
                dve.tensor_tensor(pick[:, 0:NT * NE], pick1[:, :], pick2[:, :], ALU.add).then_inc(pick_done, 1)

                def picked(dst, src, v):
                    dve.tensor_tensor(work[:, 0:NT * NE], src, v[:, :], ALU.mult)
                    dve.drain()
                    dve.tensor_reduce(dst, work[:, 0:NT * NE].rearrange("p (t e) -> p t e", t=NT), AX, ALU.add)
                    dve.drain()

                picked(s1, score[:, :], pick1)
                picked(s2, score[:, :], pick2)
                dve.tensor_tensor(ssum, s1, s2, ALU.add)
                dve.drain()
                dve.tensor_tensor(ssum, ssum, invalid, ALU.add)
                dve.drain()
                dve.reciprocal(srec, ssum)
                dve.drain()
                dve.tensor_tensor(w12[:, :, 0], s1, srec, ALU.mult)
                dve.tensor_tensor(w12[:, :, 1], s2, srec, ALU.mult)
                wait_filled(dve, "rank", l)
                dve.tensor_tensor(rcol[:, :].rearrange("p (t e) -> p t e", t=NT),
                                  bank_of("rank")[:, 0:NT * NE].rearrange("p (t e) -> p t e", t=NT),
                                  slot0.unsqueeze(1).to_broadcast([P, NT, NE]), ALU.add)
                dve.tensor_reduce(ma[:, 0:1], bank_of("rank")[:, NT * NE:(NT + 1) * NE], AX, ALU.max)
                dve.drain()
                read(dve.tensor_copy(count_max[:, :], ma[:, 0:1]), "rank")
                picked(sl1, rcol[:, :], pick1)
                picked(sl2, rcol[:, :], pick2)
                far = float(OOB)
                for j, sl in enumerate((sl1, sl2)):
                    dve.scalar_tensor_tensor(out=local[:, 0, j::2], in0=invalid, scalar=far, in1=sl, op0=ALU.mult, op1=ALU.add)
                dve.drain()
                dve.tensor_scalar(local[:, 1, :], local[:, 0, :], -float(CAP), None, ALU.add)
                dve.tensor_copy(slots[:, :], local[:, 0, :]).then_inc(slot_done, 1)
                for e in range(2):
                    dve.tensor_tensor(in_slot[:, e, :, :], iota.unsqueeze(1).to_broadcast([P, 2 * NT, P]),
                                      local[:, e, :].unsqueeze(2).to_broadcast([P, 2 * NT, P]), ALU.is_equal).then_inc(in_slot_done, 1)
                    if e == 0:
                        dve.drain()
                wait_filled(dve, "index", l)
                read(dve.tensor_reduce(first_idx[:, :], bank_of("index")[:, 0:8].rearrange("p (e b) -> p e b", e=2), AX, ALU.add), "index")
                dve.drain()
                dve.tensor_scalar(cur_res[:, :], first_idx[:, :], far, None, ALU.add)
                dve.drain()
                dve.tensor_scalar(cur_src[:, :], cur_res[:, :], 1, None, ALU.logical_shift_right).then_inc(cur_done, 2)
                split_lo(dve, l, 13)

                def rows_lo(i, s):
                    for h in range(2):
                        lo_rows(l, ("xe", s, h), h, s, hi_e, 4 * PAIRS * l + 4 * i + (2 * s + h + 1), i)

                def hidden_out(i, s):
                    wait_read(dve, ("gate", s), l, i)
                    wait_filled(dve, ("up", s), l, i)
                    read(dve.tensor_tensor(hidden[:, s, :], act_gate[:, s, :], bank_of(("up", s))[:, :], ALU.mult), ("up", s))

                def hidden_lo(i, s):
                    lo_out(dve, ("ht", s), l, xt_lo[:, 0:4, (2 + s) * P:(3 + s) * P], xt_hi[:, 0:4, (2 + s) * P:(3 + s) * P],
                           hi_h, 2 * PAIRS * l + 2 * i + (s + 1), i)

                def out1(i, s):
                    dve.wait_ge(out_free, l * NE + 2 * i + (s + 1))
                    wait_filled(dve, ("down1", s), l, i)
                    read(dve.tensor_copy(expert_out[:, s, HALF:D], bank_of(("down1", s))[:, :]), ("down1", s))

                rows_lo(0, 0)
                split_lo(dve, l, 14)
                rows_lo(0, 1)
                split_lo(dve, l, 15)

                def pair(i, last=False):
                    c = SO_MOE
                    split_lo(dve, l, c + 4, i)
                    split_lo(dve, l, c + 5, i)
                    hidden_out(i, 0)
                    split_lo(dve, l, c + 6, i)
                    split_lo(dve, l, c + 7, i)
                    split_lo(dve, l, c + 8, i)
                    split_lo(dve, l, c + 9, i)
                    hidden_lo(i, 0)
                    hidden_out(i, 1)
                    split_lo(dve, l, c + 10, i)
                    split_lo(dve, l, c + 11, i)
                    if not last:
                        rows_lo(i + 1, 0)
                        split_lo(dve, l, c, i + 1)
                    out1(i, 0)
                    hidden_lo(i, 1)
                    if not last:
                        rows_lo(i + 1, 1)
                        split_lo(dve, l, c + 1, i + 1)
                        split_lo(dve, l, c + 2, i + 1)
                    out1(i, 1)
                    if not last:
                        split_lo(dve, l, c + 3, i + 1)

                with dve.Fori(0, PAIRS - 1) as i:
                    pair(i)
                pair(PAIRS - 1, last=True)

                def block_dve(e, b, ran):
                    def lo(dst, src, hi, after):
                        dve.wait_ge(ov_act, ran * ACT_STEPS + after)
                        dve.tensor_tensor(dst, src, hi.bitcast(F32), ALU.subtract).then_inc(ov_dve, 1)

                    def unit_lo(n, after):
                        lo(w_lo[:, n % RB, :, :], raw[:, n % RB, :, :], w_hi[:, n % RB, :, :], after)

                    dve.wait_ge(ov_idx, 16 * (ran + 1))
                    dve.tensor_copy(ov_src[:, :], ov_pair[:, 1:2]).then_inc(ov_dve, 1)
                    for h in range(2):
                        lo(t_cols(xt_lo, h, 0), bank["EF"[h]][:, :].rearrange("p (k n) -> p k n", k=4), t_cols(xt_hi, h, 0), 1 + h)
                    for n in range(4):
                        unit_lo(n, 3 + n)
                    dve.wait_ge(ov_act, ran * ACT_STEPS + 7)
                    dve.wait_ge(ov_pe, ran * PE_STEPS + 4)
                    dve.tensor_tensor(hidden[:, 0, :], act_gate[:, 0, :], bank["B"][:, :], ALU.mult).then_inc(ov_dve, 1)
                    lo(xt_lo[:, 0:4, 2 * P:3 * P], bank["G"][:, :].rearrange("p (k n) -> p k n", k=4), xt_hi[:, 0:4, 2 * P:3 * P], 8)
                    for n in (4, 5):
                        unit_lo(n, 5 + n)
                    dve.wait_ge(ov_pe, ran * PE_STEPS + 7)
                    dve.tensor_copy(expert_out[:, 0, HALF:D], bank["D"][:, :]).then_inc(ov_dve, 1)

                overflow(dve, l, past, block_dve, held_dve)

                def add_second(t):
                    n = P if t < 4 else DEC
                    if t:
                        dve.wait_ge(first_added, (NT - 1) * l + t)
                    else:
                        dve.wait_ge(scaled, l + 1)
                        dve.sem_inc(held_dve, 1)
                        dve.wait_ge(y_in[0], y_count(l, 0))
                        dve.scalar_tensor_tensor(out=x[:, 0, :], in0=y_rows[:, 0, 0, :], scalar=w12[:, 0, 0:1],
                                                 in1=x[:, 0, :], op0=ALU.mult, op1=ALU.add)
                        dve.drain()
                    dve.scalar_tensor_tensor(out=x[0:n, t, :], in0=y_rows[0:n, t % YB, 1, :], scalar=w12[0:n, t, 1:2],
                                             in1=x[0:n, t, :], op0=ALU.mult, op1=ALU.add).then_inc(y_used, 1)
                    dve.drain()
                    row_stats(t).then_inc(var2_done, 1)

                def invert(t):
                    dve.wait_ge(sd2_done, NT * l + t + 1)
                    dve.reciprocal(rs[:, t:t + 1], sd[:, t:t + 1])
                    dve.drain()
                    dve.scalar_tensor_tensor(out=shift_row[:, t:t + 1], in0=mv[:, t, 0:1], scalar=-1.0, in1=rs[:, t:t + 1],
                                             op0=ALU.mult, op1=ALU.mult).then_inc(stats_done, 1)

                def gain(t):
                    dve.wait_ge(normalised, NT * l + t + 1)
                    xt = x[:, t, :].rearrange("p (a c) -> p a c", a=2)
                    ins = dve.tensor_tensor(xt, xt, table[:, 0:2, :], ALU.mult)
                    if t:
                        ins.then_inc(gained, 1)
                    else:
                        dve.drain()
                        dve.tensor_tensor(xt, xt, table[:, 2:4, :], ALU.add).then_inc(x_ready, 1)

                with dve.If(l < DEPTH - 1):
                    for s in range(RB):
                        split_lo(dve, l + 1, s)

                def tail(more):
                    dve.wait_ge(table2_in, 32 * l + 32)
                    dve.sem_inc(held_dve, 1)
                    for t in range(NT + 2):
                        if t < NT:
                            add_second(t)
                        if more and t == 1:
                            rows_lo_x(l + 1, 0)
                        if 2 <= t < NT + 1:
                            gain(t - 1)
                        if t < NT:
                            invert(t)
                        if t == 0:
                            gain(0)
                        if more and t >= 3:
                            rows_lo_x(l + 1, t - 2)

                with dve.If(l < DEPTH - 1):
                    tail(True)
                with dve.If(l > DEPTH - 2):
                    tail(False)

        @block.tensor
        def _(pe):
            for b in "ABCDEFGH":
                pe.sem_inc(freed[b], 1)
            pe.wait_ge(x0_in, 16 * 2)
            pe.sem_inc(held_pe, 1)

            def turn(name, l, srcs, i=0):
                wait_free(pe, name, l, i)
                for k, src in enumerate(srcs):
                    ins = pe.transpose(bank_of(name)[:, k * P:(k + 1) * P], src, ident)
                done(ins, name)

            def product(name, col, units, n, last=None, a_hi=xt_hi, a_lo=xt_lo):
                out = bank_of(name)[:, 0:n]
                steps = [(slot, k0 + j, j) for slot, k0 in units for j in range(4)]
                for m, (slot, k, j) in enumerate(steps):
                    for a, w in ((a_hi, w_hi), (a_hi, w_lo), (a_lo, w_hi)):
                        ins = pe.matmul(out, a[:, k, col:col + P], w[:, slot, j, 0:n],
                                        start=(m == 0 and a is a_hi and w is w_hi),
                                        stop=(m == len(steps) - 1 and a is a_lo))
                    if last is not None and m == 3:
                        ins.then_inc(half_used, 1)
                done(ins, name)

            def projection(l, g, t):
                if t == 0:
                    wait_unit(pe, l, 2 * g + 1)
                wait_free(pe, ("proj", g, t), l)
                product(("proj", g, t), t * P, [(2 * g % RB, 0), ((2 * g + 1) % RB, 4)], width(2 * g),
                        last=True if t == NT - 1 else None)

            def turn_rows(l, t):
                pe.wait_ge(x_ready, NT * l + (t + 1))
                for h in range(2):
                    turn(("xt", t, h), l, [x[:, t, (4 * h + k) * P:(4 * h + k + 1) * P] for k in range(4)])

            def head(l):
                turn_rows(l, 0)
                for t in range(NT):
                    if 2 <= t + 1 < NT:
                        turn_rows(l, t + 1)
                    wait_read(pe, ("xt", t, 1), l)
                    projection(l, 0, t)
                    if t == 0:
                        turn_rows(l, 1)

            past = new_past(pe)
            head(0)
            pe.wait_ge(boot, 16 * 4)
            pe.sem_inc(held_pe, 1)
            with pe.Fori(0, DEPTH) as l:
                for g in (1, 2, 3):
                    for t in range(NT):
                        projection(l, g, t)

                def weighted_values(t):
                    for j in range(4):
                        pe.wait_ge(exp_done, 9 * NT * l + (9 * t + 2 * j + 2))
                        turn(("pt", t, j), l, [probs[:, t % 2, j, a, b * P:(b + 1) * P] for a in range(2) for b in range(2)])
                        if j:
                            values(t, j - 1)
                    values(t, 3)

                def values(t, j):
                    if j == 0:
                        wait_free(pe, ("o", t), l)
                    wait_read(pe, ("pt", t, j), l)
                    for a in range(2):
                        h = 2 * j + a
                        c = P + h // 4 * 64
                        if t == 0:
                            v = (None, kv[:, 0, c:c + 64])
                        elif t == NT - 1:
                            v = (cache[:, 1, h // 4 * 64:h // 4 * 64 + 64], kv[:, t, c:c + 64])
                        else:
                            v = (kv[:, t - 1, c:c + 64], kv[:, t, c:c + 64])
                        for b in range(0 if t else 1, 2):
                            ins = pe.matmul(bank_of(("o", t))[:, h * 64:(h + 1) * 64], probs_t[:, j % 2, 2 * a + b, :], v[b],
                                            start=(b == (0 if t else 1)), stop=(b == 1))
                    if j == 3:
                        done(ins, ("o", t))

                def turn_queries(t):
                    turn(("qt", t), l, [q[:, t, j * P:(j + 1) * P] for j in range(4)])

                def scores(t):
                    wait_read(pe, ("qt", t), l)
                    k0 = t * P if t < NT - 1 else 5 * P
                    for j in range(4):
                        name = ("s", t, j)
                        side, jj = j % 2, j // 2
                        wait_free(pe, name, l)
                        for a in range(2):
                            for n, (qs, ks) in enumerate(((q_hi, keys_hi), (q_hi, keys_lo), (q_lo, keys_hi))):
                                ins = pe.matmul(bank_of(name)[:, a * 256:(a + 1) * 256],
                                                qs[64 * side:64 * side + 64, 2 * jj + a, :],
                                                ks[64 * side:64 * side + 64, k0:k0 + 256], start=(n == 0), stop=(n == 2))
                        done(ins, name)

                def gmlp(n):
                    name = ("gm", n)
                    wait_free(pe, name, l)
                    if n < 4:
                        ins = pe.matmul(bank_of(name)[:, :], ws_t[:, n, :], gv[:, 0:4, n * P:(n + 1) * P], start=True, stop=True)
                    else:
                        for g in range(4):
                            ins = pe.matmul(bank_of(name)[:, g * P:(g + 1) * P], ws_t[:, g, :], gv[:, 4, g * P:(g + 1) * P],
                                            start=True, stop=True)
                    done(ins, name)

                def turn_mixed(t):
                    for h, v in enumerate((q, u)):
                        pe.wait_ge(norm_done, 2 * NT * l + (2 * t + h + 1))
                        turn(("mt", t, h), l, [v[:, t, k * P:(k + 1) * P] for k in range(4)])

                def output(t):
                    wait_read(pe, ("mt", t, 1), l)
                    for c in range(2):
                        if t == 0:
                            wait_unit(pe, l, 9 + 2 * c)
                        wait_free(pe, ("wo", c, t), l)
                        product(("wo", c, t), 0, [(2 * c % RB, 0), ((2 * c + 1) % RB, 4)], HALF,
                                last=True if t == NT - 1 else None, a_hi=mt_hi, a_lo=mt_lo)

                def turn_x1(t):
                    pe.wait_ge(x1_ready, NT * l + t + 1)
                    for h in range(2):
                        turn(("rt", t, h), l, [x[:, t, (4 * h + k) * P:(4 * h + k + 1) * P] for k in range(4)])

                def expert_logits(t):
                    wait_read(pe, ("rt", t, 1), l)
                    wait_free(pe, ("logit", t), l)
                    for k in range(KT_N):
                        ins = pe.matmul(bank_of(("logit", t))[0:NE, 0:P], wrt[:, k, :], x1_t[:, k, :],
                                        start=(k == 0), stop=(k == KT_N - 1))
                    done(ins, ("logit", t))

                def turn_logits(t):
                    name = ("turned logit", t)
                    wait_read(pe, ("logit", t), l)
                    pe.sem_inc(held_pe, 1)
                    wait_free(pe, name, l)
                    pe.sem_inc(held_pe, 1)
                    done(pe.transpose(bank_of(name)[:, 0:NE], logits_t[:, :], ident[0:NE, 0:NE]), name)

                pe.wait_ge(k_done, NT * (l + 1))
                turn("kt0", l, [kv[:, t, 0:P] for t in range(4)])
                pe.wait_ge(q_done, NT * (l + 1))
                turn_queries(0)
                pe.wait_ge(ws_in, 48 * l + 48)
                turn("kt1", l, [cache[:, 0, :], kv[:, 4, 0:P]])
                pe.wait_ge(tril_done, l + 1)
                turn("wst", l, [ws[:, g, :] for g in range(4)])
                wait_read(pe, "kt1", l)
                pe.sem_inc(held_pe, 1)
                for t in range(NT + 3):
                    if t < NT:
                        scores(t)
                    if t + 1 < NT:
                        turn_queries(t + 1)
                    if t == 0:
                        wait_read(pe, "wst", l)
                        pe.sem_inc(held_pe, 1)
                        pe.wait_ge(vn_done, NT * (l + 1))
                        pe.sem_inc(held_pe, 1)
                        for r in range(NT):
                            gmlp(r)
                    if 4 <= t < NT + 2:
                        expert_logits(t - 4)
                    if t >= 3:
                        output(t - 3)
                    if 4 <= t < NT + 2:
                        turn_logits(t - 4)
                    if 1 <= t < NT + 1:
                        weighted_values(t - 1)
                    if 2 <= t < NT + 2:
                        turn_mixed(t - 2)
                    if 3 <= t < NT + 1:
                        turn_x1(t - 3)
                turn_x1(NT - 2)
                expert_logits(NT - 2)
                turn_x1(NT - 1)
                turn_logits(NT - 2)
                expert_logits(NT - 1)
                turn_logits(NT - 1)
                pe.wait_ge(pick_done, l + 1)
                wait_free(pe, "rank", l)
                pe.matmul(bank_of("rank")[:, 0:(NT + 1) * NE], before, pick[:, :], start=True, stop=False)
                for r in range(1, NT + 1):
                    ins = pe.matmul(bank_of("rank")[:, r * NE:(NT + 1) * NE], ones, pick[:, 0:(NT + 1 - r) * NE],
                                    start=False, stop=(r == NT))
                done(ins, "rank")
                wait_free(pe, "index", l)
                for e in range(2):
                    pe.wait_ge(in_slot_done, 2 * l + (e + 1))
                    for c in range(2 * NT):
                        ins = pe.matmul(bank_of("index")[:, 4 * e:4 * e + 4], in_slot[:, e, c, :], parts[:, c, :],
                                        start=(c == 0), stop=(c == 2 * NT - 1))
                done(ins, "index")

                def rows_turn(i, s):
                    pe.wait_ge(rows_in[s], 16 * (l * PAIRS + i + 1))
                    for h in range(2):
                        turn(("xe", s, h), l, [rows[:, s, (4 * h + k) * P:(4 * h + k + 1) * P] for k in range(4)], i)

                def up(i, s):
                    c = SO_MOE + 4 * s
                    for n, name in enumerate((("gate", s), ("up", s))):
                        wait_unit(pe, l, c + 2 * n + 1, i)
                        wait_free(pe, name, l, i)
                        yield product(name, s * P, [((c + 2 * n) % RB, 0), ((c + 2 * n + 1) % RB, 4)], HALF, last=True)

                def hidden_turn(i, s):
                    wait_read(pe, ("up", s), l, i)
                    turn(("ht", s), l, [hidden[:, s, k * P:(k + 1) * P] for k in range(4)], i)

                def down(i, s):
                    wait_read(pe, ("ht", s), l, i)
                    for c in range(2):
                        n = SO_MOE + 8 + 2 * s + c
                        wait_unit(pe, l, n, i)
                        wait_free(pe, (f"down{c}", s), l, i)
                        product((f"down{c}", s), (2 + s) * P, [(n % RB, 0)], HALF)

                rows_turn(0, 0)
                rows_turn(0, 1)

                def pair(i, last=False):
                    wait_read(pe, ("xe", 0, 1), l, i)
                    for _g in up(i, 0):
                        pass
                    wait_read(pe, ("xe", 1, 1), l, i)
                    second = up(i, 1)
                    next(second)
                    hidden_turn(i, 0)
                    next(second)
                    if not last:
                        rows_turn(i + 1, 0)
                    down(i, 0)
                    hidden_turn(i, 1)
                    if not last:
                        rows_turn(i + 1, 1)
                    down(i, 1)

                with pe.Fori(0, PAIRS - 1) as i:
                    pair(i)
                pair(PAIRS - 1, last=True)

                def block_pe(e, b, ran):
                    def turned(out, srcs):
                        for k, src in enumerate(srcs):
                            ins = pe.transpose(out[:, k * P:(k + 1) * P], src, ident)
                        ins.then_inc(ov_pe, 1)

                    def three_pass(out, col, units, after):
                        pe.wait_ge(ov_dve, ran * DVE_STEPS + after)
                        steps = [(slot, k0 + j, j) for slot, k0 in units for j in range(4)]
                        for m, (slot, k, j) in enumerate(steps):
                            for n, (a, w) in enumerate(((xt_hi, w_hi), (xt_hi, w_lo), (xt_lo, w_hi))):
                                ins = pe.matmul(out[:, :], a[:, k, col:col + P], w[:, slot, j, :],
                                                start=m == n == 0, stop=m == len(steps) - 1 and n == 2)
                        ins.then_inc(ov_pe, 1)

                    pe.wait_ge(ov_rows, 16 * (ran + 1))
                    for h in range(2):
                        turned(bank["EF"[h]], [rows[:, 0, (4 * h + k) * P:(4 * h + k + 1) * P] for k in range(4)])
                    three_pass(bank["A"], 0, [(0, 0), (1, 4)], 5)
                    three_pass(bank["B"], 0, [(2, 0), (3, 4)], 7)
                    pe.wait_ge(ov_dve, ran * DVE_STEPS + 8)
                    turned(bank["G"], [hidden[:, 0, k * P:(k + 1) * P] for k in range(4)])
                    for c in range(2):
                        three_pass(bank["CD"[c]], 2 * P, [(c, 0)], 10 + c)

                overflow(pe, l, past, block_pe, held_pe)

                with pe.If(l < DEPTH - 1):
                    head(l + 1)


_INS = ["x_prompt", "x_sample", "cache_k", "cache_v", "w_in", "sinks", "gm_ln_g", "gm_ln_b", "gm_ws", "gm_bs",
        "out_norm_a", "out_norm_b", "w_o", "ln1_g", "ln1_b", "w_router", "router_bias", "w_gate", "w_up", "w_down",
        "ln2_g", "ln2_b"]
_OUTS = [(1, SEQ, D), (1, DEC, D), (DEPTH, 1, P, 2, 64), (DEPTH, 1, P, 2, 64), (DEPTH, 1, DEC, 2, 64),
         (DEPTH, 1, DEC, 2, 64), (DEPTH, 1, DEC, HALF)]


def constants():
    f = np.float32
    inv = np.power(f(10000.0), -np.arange(32, dtype=f) / f(32)).astype(f)
    pos = np.concatenate([np.arange(SEQ), PAST + np.arange(DEC), np.zeros(ROWS - SEQ - DEC)]).astype(f)
    ang = (pos[:, None] * inv[None, :]).astype(np.float64)
    cos, sin = np.cos(ang), np.sin(ang)
    rope = np.stack([np.concatenate([cos, cos], 1), np.concatenate([-sin, sin], 1)], 1).astype(f)
    mask = np.zeros((3, P, 256), f)
    mask[0, 0:64, 192:] = -BIG
    mask[0, 64:, 0:64] = -BIG
    mask[1] = mask[0]
    mask[1, :, 0:P] = -BIG
    mask[2, :, 192:] = -BIG
    mats = np.zeros((P, 3 * P + 46 + 8 * NT), f)
    mats[:, 0:P] = np.triu(np.ones((P, P)), 1)
    mats[:, P:2 * P] = 1.0
    mats[:, 2 * P:3 * P] = np.arange(P)
    c = 3 * P
    mats[:, c:c + 16] = np.arange(16, 0, -1)
    mats[:, c + 16:c + 32] = CAP * np.arange(16)
    mats[:, c + 32:c + 36] = np.arange(4, 0, -1)
    mats[:, c + 36:c + 41] = 1.0
    mats[DEC:, c + 40] = 0.0
    mats[DEC:, c + 45] = 1.0
    parts = np.zeros((P, 2 * NT, 4), f)
    ints = np.zeros((P, 2 * NT, 2), np.int32)
    for t in range(NT):
        for j in range(2):
            ints[:, 2 * t + j, 0] = 2 * (t * P + np.arange(P)) + j
            ints[:, 2 * t + j, 1] = t * P + np.arange(P)
            parts[:, 2 * t + j, 0] = 2 * np.arange(P)
            parts[:, 2 * t + j, 1] = 2 * P * t
            parts[:, 2 * t + j, 2] = j
            parts[:, 2 * t + j, 3] = -OOB
    mats[:, c + 46:] = parts.reshape(P, 8 * NT)
    nowhere = np.full((NSLOT, 2), OOB, np.int32)
    return {"c_rope": rope, "c_mask": mask, "c_ident": np.eye(P, dtype=f), "c_router": mats, "c_ints": ints,
            "c_nowhere": nowhere}


def kernel(**inputs):
    import concourse.bacc as _bacc
    from concourse.bass_utils import run_bass_kernel_spmd as _run

    nc = _bacc.Bacc("TRN2", target_bir_lowering=False, num_devices=1)
    arrays, args = {}, []
    for name in _INS:
        arrays[f"in_{name}"] = np.ascontiguousarray(inputs[name])
    for name, a in constants().items():
        arrays[f"in_{name}"] = a
    for name, a in arrays.items():
        args.append(nc.dram_tensor(name, a.shape, mybir.dt.from_np(a.dtype), kind="ExternalInput").ap())
    for i, shape in enumerate(_OUTS):
        args.append(nc.dram_tensor(f"out_{i}", shape, F32, kind="ExternalOutput").ap())
    build(nc, *args)
    r = _run(nc, [arrays], core_ids=[0])
    return tuple(r.results[0][f"out_{i}"] for i in range(len(_OUTS)))
```
